# Optimizing a Trainium2 kernel written in Bass

```python
import jax, jax.numpy as jnp
from jax import lax
import numpy as np

D_MODEL = 1024
BATCH = 1
SEQ = 256
DEPTH = 1

D_FF = 2816
PLE_DIM = 256
HG_HEADS = 4
HG_KDIM = 128
HG_VDIM = 128
HG_FDIM = HG_HEADS * HG_KDIM
HG_WIDTH = HG_HEADS * HG_VDIM
CHUNK = 64
MLA_HEADS = 4
Q_LORA = 256
KV_LORA = 128
NOPE_DIM = 128
ROPE_DIM = 64
V_DIM = 128
QK_DIM = NOPE_DIM + ROPE_DIM
MLA_WIDTH = MLA_HEADS * V_DIM
QBLOCK = 128
ROPE_THETA = 10000.0
MIX_WIDTH = HG_WIDTH + MLA_WIDTH
IN_SIZES = (HG_FDIM, HG_FDIM, HG_WIDTH, HG_WIDTH, Q_LORA, KV_LORA, ROPE_DIM)
IN_WIDTH = sum(IN_SIZES)
EPS = 1e-6


def rms_norm(x, g):
    xf = x.astype(jnp.float32)
    y = xf * lax.rsqrt(jnp.mean(xf * xf, axis=-1, keepdims=True) + EPS)
    return (y * g.astype(jnp.float32)).astype(x.dtype)

def swiglu(x, w_gate, w_up, w_down):
    return (jax.nn.silu(x @ w_gate) * (x @ w_up)) @ w_down

def apply_rope(x, cos, sin):
    x1, x2 = jnp.split(x.astype(jnp.float32), 2, axis=-1)
    return jnp.concatenate([x1 * cos - x2 * sin, x2 * cos + x1 * sin], axis=-1).astype(x.dtype)

def hgrn2_chunkwise(q, log_f, k, v):
    B, S, H, DK = q.shape
    DV = v.shape[-1]
    n_chunks = S // CHUNK

    def to_chunks(t):
        return t.reshape(B, n_chunks, CHUNK, H, t.shape[-1]).transpose(1, 0, 3, 2, 4)

    causal = jnp.tril(jnp.ones((CHUNK, CHUNK), dtype=bool))[:, :, None]

    def step(state, inp):
        q_c, g_c, k_c, v_c = inp
        b = jnp.cumsum(g_c, axis=2)
        diff = b[:, :, :, None, :] - b[:, :, None, :, :]
        decay = jnp.exp(jnp.where(causal, diff, -jnp.inf))
        scores = jnp.einsum('bhtd,bhsd,bhtsd->bhts', q_c, k_c, decay)
        o = (jnp.einsum('bhts,bhsv->bhtv', scores, v_c)
             + jnp.einsum('bhtd,bhdv->bhtv', q_c * jnp.exp(b), state))
        b_last = b[:, :, -1:, :]
        state = (state * jnp.exp(b_last)[:, :, 0, :, None]
                 + jnp.einsum('bhsd,bhsv->bhdv', k_c * jnp.exp(b_last - b), v_c))
        return state, o

    s0 = jnp.zeros((B, H, DK, DV), jnp.float32)
    _, o = lax.scan(step, s0, tuple(map(to_chunks, (q, log_f, k, v))))
    return o.transpose(1, 0, 3, 2, 4).reshape(B, S, H, DV)

def causal_block_attention(q, k, v):
    S = q.shape[2]
    scale = QK_DIM ** -0.5
    outs = []
    for j in range(S // QBLOCK):
        lo, hi = j * QBLOCK, (j + 1) * QBLOCK
        s = jnp.einsum('bhqd,bhkd->bhqk', q[:, :, lo:hi], k[:, :, :hi]).astype(jnp.float32) * scale
        mask = (lo + jnp.arange(QBLOCK))[:, None] >= jnp.arange(hi)[None, :]
        s = jnp.where(mask, s, -jnp.inf)
        pr = jax.nn.softmax(s, axis=-1).astype(v.dtype)
        outs.append(jnp.einsum('bhqk,bhkv->bhqv', pr, v[:, :, :hi]))
    return jnp.concatenate(outs, axis=2)

def first_inputs(seed: int = 0) -> dict:
    key = jax.random.key(seed)
    ks = jax.random.split(key, 24)

    def w(k, shape, fan_in):
        return jax.random.normal(k, shape, jnp.float32) * fan_in ** -0.5

    def gain(k, shape):
        return 1.0 + 0.02 * jax.random.normal(k, shape, jnp.float32)

    offsets = jax.random.randint(ks[2], (BATCH, 1), 0, 1024, dtype=jnp.int32)
    positions = offsets + jnp.arange(SEQ, dtype=jnp.int32)[None, :]
    return {
        "x": jax.random.normal(ks[0], (BATCH, SEQ, D_MODEL), jnp.float32),
        "p": jax.random.normal(ks[1], (DEPTH, BATCH, SEQ, PLE_DIM), jnp.float32),
        "positions": positions,
        "ln_ffn1": gain(ks[3], (DEPTH, D_MODEL)),
        "w1_gate": w(ks[4], (DEPTH, D_MODEL, D_FF), D_MODEL),
        "w1_up": w(ks[5], (DEPTH, D_MODEL, D_FF), D_MODEL),
        "w1_down": w(ks[6], (DEPTH, D_FF, D_MODEL), D_FF),
        "ln_mix": gain(ks[7], (DEPTH, D_MODEL)),
        "w_in": w(ks[8], (DEPTH, D_MODEL, IN_WIDTH), D_MODEL),
        "hg_lb_logits": 0.5 * jax.random.normal(ks[9], (DEPTH + 1, HG_FDIM), jnp.float32),
        "hg_out_norm": gain(ks[10], (DEPTH, HG_HEADS, HG_VDIM)),
        "q_a_norm": gain(ks[11], (DEPTH, Q_LORA)),
        "w_q_up": w(ks[12], (DEPTH, Q_LORA, MLA_HEADS * QK_DIM), Q_LORA),
        "kv_a_norm": gain(ks[13], (DEPTH, KV_LORA)),
        "w_kv_up": w(ks[14], (DEPTH, KV_LORA, MLA_HEADS * (NOPE_DIM + V_DIM)), KV_LORA),
        "w_out": w(ks[15], (DEPTH, MIX_WIDTH, D_MODEL), MIX_WIDTH),
        "ln_ffn2": gain(ks[16], (DEPTH, D_MODEL)),
        "w2_gate": w(ks[17], (DEPTH, D_MODEL, D_FF), D_MODEL),
        "w2_up": w(ks[18], (DEPTH, D_MODEL, D_FF), D_MODEL),
        "w2_down": w(ks[19], (DEPTH, D_FF, D_MODEL), D_FF),
        "ln_ple": gain(ks[20], (DEPTH, D_MODEL)),
        "w_ple_gate": w(ks[21], (DEPTH, D_MODEL, D_MODEL), D_MODEL),
        "w_ple_proj": w(ks[22], (DEPTH, PLE_DIM, D_MODEL), PLE_DIM),
        "ln_final": gain(ks[23], (D_MODEL,)),
    }

def first_block(x, p, positions, ln_ffn1, w1_gate, w1_up, w1_down, ln_mix, w_in,
              hg_lb_logits, hg_out_norm, q_a_norm, w_q_up, kv_a_norm, w_kv_up, w_out,
              ln_ffn2, w2_gate, w2_up, w2_down, ln_ple, w_ple_gate, w_ple_proj, ln_final):
    B, S, _ = x.shape
    split_at = [int(v) for v in np.cumsum(IN_SIZES)[:-1]]

    lower_bounds = jnp.cumsum(jax.nn.softmax(hg_lb_logits.astype(jnp.float32), axis=0), axis=0)

    half = ROPE_DIM // 2
    inv_freq = ROPE_THETA ** (-jnp.arange(half, dtype=jnp.float32) / half)
    ang = positions.astype(jnp.float32)[..., None] * inv_freq
    cos, sin = jnp.cos(ang), jnp.sin(ang)

    h = x
    for i in range(DEPTH):
        h = h + 0.5 * swiglu(rms_norm(h, ln_ffn1[i]), w1_gate[i], w1_up[i], w1_down[i])

        u = rms_norm(h, ln_mix[i]) @ w_in[i]
        hq, hf, hi_, hg, cq, ckv, kr = jnp.split(u, split_at, axis=-1)

        lb = lower_bounds[i]
        f_raw = hf.astype(jnp.float32)
        log_f = jnp.log(lb + (1.0 - lb) * jax.nn.sigmoid(f_raw))
        k_in = (1.0 - lb) * jax.nn.sigmoid(-f_raw)
        o_hg = hgrn2_chunkwise(
            hq.astype(jnp.float32).reshape(B, S, HG_HEADS, HG_KDIM),
            log_f.reshape(B, S, HG_HEADS, HG_KDIM),
            k_in.reshape(B, S, HG_HEADS, HG_KDIM),
            hi_.astype(jnp.float32).reshape(B, S, HG_HEADS, HG_VDIM)).astype(h.dtype)
        o_hg = rms_norm(o_hg, hg_out_norm[i]).reshape(B, S, HG_WIDTH) * jax.nn.silu(hg)

        q = (rms_norm(cq, q_a_norm[i]) @ w_q_up[i]).reshape(B, S, MLA_HEADS, QK_DIM)
        q_nope, q_rope = jnp.split(q, [NOPE_DIM], axis=-1)
        q_rope = apply_rope(q_rope, cos[:, :, None, :], sin[:, :, None, :])
        kv = (rms_norm(ckv, kv_a_norm[i]) @ w_kv_up[i]).reshape(B, S, MLA_HEADS, NOPE_DIM + V_DIM)
        k_nope, v = jnp.split(kv, [NOPE_DIM], axis=-1)
        k_rope = apply_rope(kr, cos, sin)
        k_rope = jnp.broadcast_to(k_rope[:, :, None, :], (B, S, MLA_HEADS, ROPE_DIM))
        qf = jnp.concatenate([q_nope, q_rope], axis=-1).transpose(0, 2, 1, 3)
        kf = jnp.concatenate([k_nope, k_rope], axis=-1).transpose(0, 2, 1, 3)
        o_mla = causal_block_attention(qf, kf, v.transpose(0, 2, 1, 3))
        o_mla = o_mla.transpose(0, 2, 1, 3).reshape(B, S, MLA_WIDTH)

        h = h + jnp.concatenate([o_hg, o_mla], axis=-1) @ w_out[i]

        h = h + 0.5 * swiglu(rms_norm(h, ln_ffn2[i]), w2_gate[i], w2_up[i], w2_down[i])

        gate = jax.nn.sigmoid(rms_norm(h, ln_ple[i]) @ w_ple_gate[i])
        h = h + gate * (p[i].astype(h.dtype) @ w_ple_proj[i])

    return rms_norm(h, ln_final)


POOL_GROUPS = 4
POOL_WINDOWS = (2, 4, 8, 16)
POOL_GROUP_W = 128
POOL_W = POOL_GROUPS * POOL_GROUP_W
POOL_OUT_GROUP_W = D_MODEL // POOL_GROUPS
ATTN_HEADS = 16
HEAD_DIM = 64
ATTN_W = ATTN_HEADS * HEAD_DIM
Q_BLOCK = 128
N_BRANCH = 2
IN_W = POOL_W + 3 * ATTN_W + ATTN_HEADS + N_BRANCH * D_MODEL
PEER_HEADS = 8
N_KEYS = 128
N_EXPERTS = N_KEYS * N_KEYS
PEER_HALF = 128
PEER_KEY_DIM = 2 * PEER_HALF
PEER_TOPK = 16
TOK_CHUNK = 128
N_MOD = 6
NEG_INF = -1e30


def rmsnorm(x, g):
    xf = x.astype(jnp.float32)
    y = xf * lax.rsqrt(jnp.mean(xf * xf, axis=-1, keepdims=True) + EPS)
    return (y * g.astype(jnp.float32)).astype(x.dtype)

def modulate(h, shift, scale):
    return h * (1.0 + scale[:, None, :]) + shift[:, None, :]

def causal_pool_mixer(u, w_pool, pool_scale):
    B, S, _ = u.shape
    ug = u.reshape(B, S, POOL_GROUPS, POOL_GROUP_W)
    cs = jnp.cumsum(ug.astype(jnp.float32), axis=1)
    pos = jnp.arange(S)
    means = []
    for g, w in enumerate(POOL_WINDOWS):
        csg = cs[:, :, g]
        lag = jnp.pad(csg, ((0, 0), (w, 0), (0, 0)))[:, :S]
        cnt = jnp.minimum(pos + 1, w).astype(jnp.float32)[None, :, None]
        means.append((csg - lag) / cnt)
    pooled = jnp.stack(means, axis=2).astype(u.dtype) - ug
    y = jnp.einsum('bsgc,gcd->bsgd', pooled, w_pool).reshape(B, S, D_MODEL)
    return y * pool_scale

def forgetting_attention(q, k, v, log_f):
    B, S, H, Dh = q.shape
    F = jnp.transpose(jnp.cumsum(log_f.astype(jnp.float32), axis=1), (0, 2, 1))
    scale = Dh ** -0.5
    outs = []
    for i in range(S // Q_BLOCK):
        q0 = i * Q_BLOCK
        L = q0 + Q_BLOCK
        s = jnp.einsum('bqhd,bkhd->bhqk', q[:, q0:L], k[:, :L],
                       preferred_element_type=jnp.float32) * scale
        s = s + F[:, :, q0:L, None] - F[:, :, None, :L]
        qpos = q0 + jnp.arange(Q_BLOCK)
        kpos = jnp.arange(L)
        s = jnp.where(kpos[None, :] <= qpos[:, None], s, NEG_INF)
        p = jax.nn.softmax(s, axis=-1).astype(v.dtype)
        outs.append(jnp.einsum('bhqk,bkhd->bqhd', p, v[:, :L]))
    return jnp.concatenate(outs, axis=1).reshape(B, S, H * Dh)

def peer_ffn(h, w_query, sub_keys, expert_u, expert_v):
    B, S, D = h.shape
    q = jnp.einsum('bsd,dk->bsk', h, w_query).reshape(B, S, PEER_HEADS, 2, PEER_HALF)
    sc = jnp.einsum('bshpc,hpnc->bshpn', q, sub_keys,
                    preferred_element_type=jnp.float32)
    s1, i1 = lax.top_k(sc[..., 0, :], PEER_TOPK)
    s2, i2 = lax.top_k(sc[..., 1, :], PEER_TOPK)
    cand_s = (s1[..., :, None] + s2[..., None, :]).reshape(B, S, PEER_HEADS, PEER_TOPK * PEER_TOPK)
    cand_i = (i1[..., :, None] * N_KEYS + i2[..., None, :]).reshape(B, S, PEER_HEADS, PEER_TOPK * PEER_TOPK)
    top_s, sel = lax.top_k(cand_s, PEER_TOPK)
    idx = jnp.take_along_axis(cand_i, sel, axis=-1)
    gates = jax.nn.softmax(top_s, axis=-1).astype(h.dtype)
    T = B * S
    n_chunks = T // TOK_CHUNK
    hc = h.reshape(n_chunks, TOK_CHUNK, D)
    ic = idx.reshape(n_chunks, TOK_CHUNK, PEER_HEADS, PEER_TOPK)
    gc = gates.reshape(n_chunks, TOK_CHUNK, PEER_HEADS, PEER_TOPK)

    def chunk(args):
        xc, ec, wc = args
        u = expert_u[ec]
        a = jax.nn.gelu(jnp.einsum('cd,chkd->chk', xc, u), approximate=False) * wc
        return jnp.einsum('chk,chkd->cd', a, expert_v[ec])

    out = lax.map(chunk, (hc, ic, gc))
    return out.reshape(B, S, D)

def second_inputs(seed: int = 0) -> dict:
    key = jax.random.key(seed)
    ks = jax.random.split(key, 20)
    nrm = jax.random.normal
    d = D_MODEL
    x = nrm(ks[0], (BATCH, SEQ, d), jnp.float32)
    c = nrm(ks[1], (BATCH, d), jnp.float32)
    w_mod = nrm(ks[2], (DEPTH, d, N_MOD * d), jnp.float32) * (0.5 * d ** -0.5)
    b_mod = nrm(ks[3], (DEPTH, N_MOD * d), jnp.float32) * 0.02
    norm1_g = 1.0 + 0.02 * nrm(ks[4], (DEPTH, d), jnp.float32)
    w_in = nrm(ks[5], (DEPTH, d, IN_W), jnp.float32) * d ** -0.5
    b_f = jax.random.uniform(ks[6], (DEPTH, ATTN_HEADS), jnp.float32, 1.0, 4.0)
    w_pool = nrm(ks[7], (DEPTH, POOL_GROUPS, POOL_GROUP_W, POOL_OUT_GROUP_W), jnp.float32) * POOL_GROUP_W ** -0.5
    pool_scale = 1.0 + 0.02 * nrm(ks[8], (DEPTH, d), jnp.float32)
    w_out = nrm(ks[9], (DEPTH, d, d), jnp.float32) * d ** -0.5
    norm2_g = 1.0 + 0.02 * nrm(ks[10], (DEPTH, d), jnp.float32)
    peer_w_query = nrm(ks[11], (DEPTH, d, PEER_HEADS * PEER_KEY_DIM), jnp.float32) * d ** -0.5
    peer_sub_keys = nrm(ks[12], (DEPTH, PEER_HEADS, 2, N_KEYS, PEER_HALF), jnp.float32) * PEER_HALF ** -0.5
    peer_u = nrm(ks[13], (DEPTH, N_EXPERTS, d), jnp.float32) * d ** -0.5
    peer_v = nrm(ks[14], (DEPTH, N_EXPERTS, d), jnp.float32) * PEER_HEADS ** -0.5
    final_g = 1.0 + 0.02 * nrm(ks[15], (d,), jnp.float32)
    return {"x": x, "c": c, "w_mod": w_mod, "b_mod": b_mod, "norm1_g": norm1_g,
            "w_in": w_in, "b_f": b_f, "w_pool": w_pool, "pool_scale": pool_scale,
            "w_out": w_out, "norm2_g": norm2_g, "peer_w_query": peer_w_query,
            "peer_sub_keys": peer_sub_keys, "peer_u": peer_u, "peer_v": peer_v,
            "final_g": final_g}

def second_block(x, c, w_mod, b_mod, norm1_g, w_in, b_f, w_pool, pool_scale, w_out,
              norm2_g, peer_w_query, peer_sub_keys, peer_u, peer_v, final_g):
    B, S, D = x.shape
    for l in range(DEPTH):
        mod = jnp.einsum('bd,de->be', c, w_mod[l]) + b_mod[l]
        sh1, sc1, gt1, sh2, sc2, gt2 = jnp.split(mod, N_MOD, axis=-1)

        h = modulate(rmsnorm(x, norm1_g[l]), sh1, sc1)
        z = jnp.einsum('bsd,de->bse', h, w_in[l])
        o = 0
        u_pool = z[..., o:o + POOL_W]; o += POOL_W
        q = z[..., o:o + ATTN_W].reshape(B, S, ATTN_HEADS, HEAD_DIM); o += ATTN_W
        k = z[..., o:o + ATTN_W].reshape(B, S, ATTN_HEADS, HEAD_DIM); o += ATTN_W
        v = z[..., o:o + ATTN_W].reshape(B, S, ATTN_HEADS, HEAD_DIM); o += ATTN_W
        f_logit = z[..., o:o + ATTN_HEADS]; o += ATTN_HEADS
        g_a = jax.nn.sigmoid(z[..., o:o + D]); o += D
        g_b = jax.nn.sigmoid(z[..., o:o + D])

        y_a = causal_pool_mixer(u_pool, w_pool[l], pool_scale[l])
        log_f = jax.nn.log_sigmoid((f_logit + b_f[l]).astype(jnp.float32))
        y_b = forgetting_attention(q, k, v, log_f)
        y = g_a * y_a + g_b * y_b
        x = x + gt1[:, None, :] * jnp.einsum('bsd,de->bse', y, w_out[l])

        h2 = modulate(rmsnorm(x, norm2_g[l]), sh2, sc2)
        x = x + gt2[:, None, :] * peer_ffn(h2, peer_w_query[l], peer_sub_keys[l], peer_u[l], peer_v[l])
    return rmsnorm(x, final_g)


def setup_inputs(seed=0):
    out = dict(first_inputs(seed))
    for name, value in second_inputs(seed + 1).items():
        if name != "x":
            out[name + "_2"] = value
    return out


def reference(
    x, p, positions, ln_ffn1, w1_gate, w1_up, w1_down, ln_mix, w_in, hg_lb_logits, hg_out_norm,
    q_a_norm, w_q_up, kv_a_norm, w_kv_up, w_out, ln_ffn2, w2_gate, w2_up, w2_down, ln_ple,
    w_ple_gate, w_ple_proj, ln_final, c_2, w_mod_2, b_mod_2, norm1_g_2, w_in_2, b_f_2, w_pool_2,
    pool_scale_2, w_out_2, norm2_g_2, peer_w_query_2, peer_sub_keys_2, peer_u_2, peer_v_2,
    final_g_2,
):
    x = first_block(
        x, p, positions, ln_ffn1, w1_gate, w1_up, w1_down, ln_mix, w_in, hg_lb_logits,
        hg_out_norm, q_a_norm, w_q_up, kv_a_norm, w_kv_up, w_out, ln_ffn2, w2_gate, w2_up,
        w2_down, ln_ple, w_ple_gate, w_ple_proj, ln_final,
    )
    return second_block(
        x, c_2, w_mod_2, b_mod_2, norm1_g_2, w_in_2, b_f_2, w_pool_2, pool_scale_2, w_out_2,
        norm2_g_2, peer_w_query_2, peer_sub_keys_2, peer_u_2, peer_v_2, final_g_2,
    )


_drawn_inputs = setup_inputs


def setup_inputs(seed=0):
    import zlib

    import numpy as np

    out = dict(_drawn_inputs(seed))
    spreads = {}
    factors = {'ln_ffn1': 4.16,
     'ln_mix': 2.889,
     'hg_out_norm': 4.942,
     'q_a_norm': 8.0,
     'kv_a_norm': 7.815,
     'ln_ffn2': 5.098,
     'ln_ple': 64.0,
     'norm1_g_2': 4.739,
     'pool_scale_2': 6.008,
     'norm2_g_2': 31.832,
     'final_g_2': 7.905}
    for name, (base, spread) in spreads.items():
        noise = np.random.default_rng([zlib.crc32(name.encode()), seed]).standard_normal(out[name].shape)
        drawn = base * np.exp(spread * noise) if base else spread * noise
        out[name] = __import__('jax').numpy.asarray(drawn.astype(out[name].dtype))
    for name, factor in factors.items():
        out[name] = (out[name] * factor).astype(out[name].dtype)
    return out
```

```python
from contextlib import ExitStack

import numpy as np

import concourse.bass as bass
from concourse import mybir

P = 128
T = 256
TB = T // P
D = 1024
C = D // P
FF = 2816
FC = FF // P
FB = FF // T
HH = 4
ROPE = 64
QK = 128 + ROPE
AH = 16
AD = 64
PH = 8
NK = 128
TK = 16
EPS = 1e-6
SLOT8 = C * T
SLOT22 = FC * P
RING = 4
MODS = 6 * D // T
MOD_RING = 2
NEG = -3.0e38
LEVELS = 7
RU = 8
RV = 8
UB = 4
UNITS = PH * TB
ARENA = 20400
AHEAD = 2

F32 = mybir.dt.float32
I32 = mybir.dt.int32
U32 = mybir.dt.uint32
ALU = mybir.AluOpType
ACT = mybir.ActivationFunctionType
AX = mybir.AxisListType.X

S_FFN1 = 0
S_DOWN1 = S_FFN1 + 2 * FB
S_IN = S_DOWN1 + C
N_IN = 10
S_OUT = S_IN + N_IN
S_FFN2 = S_OUT + 4
S_DOWN2 = S_FFN2 + 2 * FB
S_PLE = S_DOWN2 + C
S_IN2 = S_PLE + 4
N_IN2 = 22
S_OUT2 = S_IN2 + N_IN2
S_PQ = S_OUT2 + 4
S_END = S_PQ + PH


def columns(widths):
    at, out = 0, {}
    for name, width in widths:
        out[name] = (at, at + width)
        at += width
    return out, at


VEC, N_VEC = columns([("ffn1", C), ("mix", C), ("ffn2", C), ("ple", C), ("final1", C), ("norm1", C),
                      ("norm2", C), ("pool_scale", C), ("hg_norm", HH), ("q_a", 2), ("kv_a", 1),
                      ("lb", 2 * HH), ("c", C), ("b_mod", 6 * C), ("b_f", 1)])
CON, N_CON = columns([("ident", P), ("swap", ROPE), ("causal", 2 * P), ("iota", TK), ("inv_freq", 1),
                      ("is_value", 1), ("not_value", 1), ("sel_q", AH), ("sel_k", AH)])
SMALL, N_SMALL = columns([("w_q_up", 2 * HH * QK), ("w_kv_up", HH * 2 * P), ("w_ple", 2 * D),
                          ("w_pool", 4 * T)])


class Chain:

    def __init__(self, eng, sem, apart):
        self.eng, self.sem, self.waited, self.n, self.turn = eng, sem, apart, 0, 0

    def __call__(self, ins, apart=False):
        self.n += 1
        ins.then_inc(self.sem, 1)
        self.eng.wait_ge(self.sem, self.turn + self.n)
        if apart:
            self.apart()

    def apart(self):
        self.eng.sem_inc(self.waited, 1)

    def loop(self, i, per):
        self.turn, self.start, self.per = i * per, self.n, per

    def end(self, turns):
        assert self.n - self.start == self.per, (self.n - self.start, self.per)
        self.n, self.turn = self.start + turns * self.per, 0


def program(nc, a, out):
    with ExitStack() as ctx:
        sems = {}

        def S(name):
            if name not in sems:
                sems[name] = ctx.enter_context(nc.semaphore(name))
            return sems[name]

        def sb(name, shape, dt=F32):
            return ctx.enter_context(nc.sbuf_tensor(name, shape, dt))

        ps = ctx.enter_context(nc.psum_tensor("ps", [P, 8, 512], F32))
        ring = sb("ring", [P, RING, SLOT22])
        vec = sb("vec", [P, N_VEC])
        con = sb("con", [P, N_CON])
        small = sb("small", [P, N_SMALL])
        keys = sb("keys", [P, 2 * PH, P])
        wf = sb("wf", [P, C, 96])
        lev_mask = sb("lev_mask", [P, LEVELS + 1, P], I32)
        inv_count = sb("inv_count", [P, 4, T])
        h = sb("h", [P, C, T])
        nrm = sb("nrm", [P, C, T])
        sq = sb("sq", [P, C, T])
        ones = sb("ones", [P, P])
        zeros = sb("zeros", [P, P])
        pT = sb("pT", [P, 2, T])
        eps = sb("eps", [P, 1])
        std = sb("std", [P, 2, T])
        rstd = sb("rstd", [P, 2, T])
        mod = sb("mod", [P, 6 * C])
        coef = sb("coef", [P, 2 * C])
        silu = sb("silu", [P, 2, T])
        lb = sb("lb", [P, 8, HH])
        ang = sb("ang", [ROPE, 4, T])
        posi = sb("posi", [ROPE, T], I32)
        cos = sb("cos", [ROPE, T])
        sin = sb("sin", [ROPE, T])
        arena = sb("arena", [P, ARENA])

        def carve(widths):
            at, views = 0, {}
            for name, width in widths:
                views[name] = arena[:, at:at + width]
                at += width
            assert at <= ARENA, at
            return views

        def heads(ap, n):
            return ap.rearrange("p (h t) -> p h t", h=n)

        def V(name, j=0, n=1):
            lo = VEC[name][0] + j
            return vec[:, lo:lo + n]

        def K(name, rows=P):
            lo, hi = CON[name]
            return con[0:rows, lo:hi]

        ident = K("ident")
        w_q_up = small[:, slice(*SMALL["w_q_up"])].rearrange("p (k n) -> p k n", k=2)
        w_kv_up = small[:, slice(*SMALL["w_kv_up"])].rearrange("p (h n) -> p h n", h=HH)
        w_ple = small[:, slice(*SMALL["w_ple"])].rearrange("p (k n) -> p k n", k=2)
        w_pool = small[:, slice(*SMALL["w_pool"])].rearrange("p (g n) -> p g n", g=4)

        ff = carve([("gu", FC * T), ("wm", MOD_RING * SLOT8), ("sum", RING * T)])
        gu = heads(ff["gu"], FC)
        wm = ff["wm"].rearrange("p (r k n) -> p r k n", r=MOD_RING, k=C)
        mod_sum = heads(ff["sum"], RING)

        m = carve([("q", 1024), ("k", 1024), ("qf", 1024), ("sc", 1024), ("sc7", 512), ("b0", 1024),
                   ("b1", 1024), ("v", 1024), ("g", 1024), ("o", 1024), ("cq", 768), ("cqn", 768), ("xr", 1280),
                   ("rot", 1280),
                   ("qn", 1024), ("kn", 1024), ("va", 1024), ("pr", 1536), ("prT", 1536),
                   ("st", 64)])
        hq, hk, hqf = heads(m["q"], HH), heads(m["k"], HH), heads(m["qf"], HH)
        scT = m["sc"].rearrange("p (h b t) -> p h b t", h=HH, b=TB)
        sc7 = heads(m["sc7"], HH)
        hv = m["v"].rearrange("p (b n) -> p b n", b=TB)
        hg, ho = heads(m["g"], HH), heads(m["o"], HH)
        csq, osq, ostd = sq[:, 0:3, :], sq[:, 0:HH, :], sq[:, HH:C, :]
        cq, cqn = heads(m["cq"], 3), heads(m["cqn"], 3)
        xr, rot, rt = (heads(x, HH + 1) for x in (m["xr"], m["rot"], m["prT"][:, 0:(HH + 1) * T]))
        qn, kn = heads(m["qn"], HH), heads(m["kn"], HH)
        va = m["va"].rearrange("p (b n) -> p b n", b=TB)
        mixed = nrm

        s = carve([("qp", AH * T), ("kp", AH * T), ("v", TB * D), ("ga", C * T), ("gb", C * T),
                   ("pool", 4 * T), ("pr", 1536), ("prT", 1536), ("st", 64), ("f", 6 * T)])
        qp, kp = heads(s["qp"], AH), heads(s["kp"], AH)
        v2 = s["v"].rearrange("p (b n) -> p b n", b=TB)
        ga, gb, o2 = heads(s["ga"], C), heads(s["gb"], C), sq
        at = 0
        for name, groups in (("up", 4), ("s1", 4), ("s2", 3), ("s4", 2), ("s8", 1)):
            s[name] = small[:, at:at + groups * 272]
            at += groups * 272
        up, s1, s2, s4, s8 = (s[x].rearrange("p (g t) -> p g t", t=272) for x in ("up", "s1", "s2", "s4", "s8"))
        pooled = heads(s["pool"], 4)
        fl = heads(s["f"], 6)

        e = carve([("qT", 4 * T), ("U", RU * D), ("V", RV * D), ("junk", D), ("wk", 3 * 256), ("oh", 2 * 256), ("vals", UB * 64), ("sel", 32),
                   ("few", UB * 96)])
        qT = heads(e["qT"], 4)
        h2 = sq[:, :, :].rearrange("p c t -> p (c t)").rearrange("p (b n) -> p b n", b=TB)
        gtrow, fgrow = small[:, PH * 512:PH * 512 + D], lev_mask[:, :, :].rearrange("p l t -> p (l t)").bitcast(F32)
        gtb = inv_count[:, :, :].rearrange("p g t -> p (g t)").rearrange("p (c t) -> p c t", c=C)
        ubuf, vbuf = heads(e["U"], RU), heads(e["V"], RV)
        diag = nrm[:, :, :].rearrange("p c t -> p (c t)").rearrange("p (k t) -> p k t", k=TK)
        scores = small[:, 0:PH * 512].rearrange("p (h b n) -> p h b n", h=PH, b=TB)

        def pair(r):
            return ps[:, r, :].rearrange("p (t n) -> p t n", t=2)

        def slot8(r):
            return ring[:, r, 0:SLOT8].rearrange("p (k n) -> p k n", k=C)

        def slot22(r):
            return ring[:, r, :].rearrange("p (k n) -> p k n", k=FC)

        block = ctx.enter_context(nc.Block())

        @block.sync
        def _(sp):
            def load(src, at, slot, turn=0, free=True):
                r = slot % RING
                if free:
                    sp.wait_ge(S("slots_done"), turn + (slot - RING + 1))
                words = src.shape[2]
                sp.dma_start(ring[:, r, 0:words], row(src, at)).then_inc(S(f"landed{r}"), 16)

            def row(src, at):
                return src[at, :, :] if isinstance(at, int) else src[bass.ds(at, 1), :, :].rearrange("a p n -> p (a n)")

            def load_mod(j, turn=0, free=True):
                r = j % MOD_RING
                if free:
                    sp.wait_ge(S("mod_summed"), turn + (j - MOD_RING + 1))
                sp.dma_start(wm[:, r, :, :].rearrange("p k n -> p (k n)"), row(a["wmod"], turn + j)
                             ).then_inc(S(f"mod_landed{r}"), 16)

            def stream(src, at, slot, n):
                turns = n // RING
                with sp.Fori(0, turns) as i:
                    for j in range(RING):
                        load(src, i * RING + (at + j), slot + j, i * RING)
                for j in range(turns * RING, n):
                    load(src, at + j, slot + j)

            for j in range(RING):
                load(a["w8"], j, j, free=False)
            for j in range(MOD_RING):
                load_mod(j, free=False)
            turns = (2 * FB - RING) // RING
            with sp.Fori(0, turns) as i:
                for j in range(RING):
                    load(a["w8"], i * RING + (RING + j), RING + j, i * RING)
                    load_mod(MOD_RING + j, i * RING)
            mods = MOD_RING + turns * RING
            for j in range((turns + 1) * RING, 2 * FB):
                load(a["w8"], j, j)
                load_mod(mods)
                mods += 1
            for j in range(C):
                load(a["w22"], j, S_DOWN1 + j)
                if mods < MODS:
                    load_mod(mods)
                    mods += 1
            at = S_DOWN1
            n = S_DOWN2 - S_IN
            stream(a["w8"], at, S_IN, n)
            at += n
            stream(a["w22"], C, S_DOWN2, C)
            stream(a["w8"], at, S_PLE, S_END - S_PLE)
            for b in range(TB):
                sp.wait_ge(S("out_ready"), b + 1)
                sp.dma_start(out[b * P:(b + 1) * P, :], ubuf[:, b, :]).then_inc(S("stored"), 16)
            sp.wait_ge(S("stored"), 16 * TB)

        @block.tensor
        def _(pe):
            mm = nc.tensor.matmul

            def begin(slot, turn=0):
                pe.wait_ge(S(f"landed{slot % RING}"), turn * 4 + 16 * (slot // RING + 1))
                if slot >= RING:
                    pe.wait_ge(S("banks_freed"), turn + (slot - RING + 1))

            def features(slot, x, turn=0, n_at=None, tiles=((0, P), (P, P))):
                r = slot % RING
                begin(slot, turn)
                for t, (lo, width) in enumerate(tiles):
                    for k in range(C):
                        if n_at is not None and t == 0:
                            pe.wait_ge(S("normed"), n_at + k + 1)
                        last = mm(pair(r)[0:width, t, :], slot8(r)[:, k, lo:lo + width], x[:, k, :],
                                  start=(k == 0), stop=(k == C - 1))
                last.then_inc(S("slots_done"), 1)

            def tokens(slot, x):
                r = slot % RING
                begin(slot)
                for b in range(TB):
                    for k in range(C):
                        last = mm(pair(r)[:, b, :], x[:, k, b * P:(b + 1) * P], slot8(r)[:, k, :],
                                  start=(k == 0), stop=(k == C - 1))
                last.then_inc(S("slots_done"), 1)

            def modulation(n, turn=0):
                pe.wait_ge(S("mod_summed"), turn + (n + RING))
                for j in range(2 * RING):
                    to = ps[:, 5, 2 * n + j:2 * n + j + 1] if isinstance(turn, int) else \
                        ps[:, 5, bass.ds(turn * 2 + (2 * n + j), 1)]
                    last = mm(to, mod_sum[:, j // 2, (j % 2) * P:(j % 2 + 1) * P], ones[:, 0:1], start=True, stop=True)
                last.then_inc(S("mod_read"), 1)

            def square_sum(m, c):
                pe.wait_ge(S("squared"), m * C + c + 1)
                if c == 0 and m:
                    pe.wait_ge(S("std_ready"), m)
                last = mm(ps[:, 4, 0:T], ones[:, :], sq[:, c, :], start=(c == 0), stop=(c == C - 1))
                if c == C - 1:
                    last.then_inc(S("sum_ready"), 1)

            def down(slot, m, mods=None):
                for j in range(C):
                    r = (slot + j) % RING
                    begin(slot + j)
                    if j == 0:
                        pe.wait_ge(S("banks_freed"), slot)
                    for k in range(FC):
                        last = mm(ps[:, r, 0:T], slot22(r)[:, k, :], gu[:, k, :],
                                  start=(k == 0), stop=(k == FC - 1))
                    last.then_inc(S("slots_done"), 1)
                    if mods is not None and j == C - 1:
                        modulation(mods)
                    if j >= 2:
                        square_sum(m, j - 2)
                square_sum(m, C - 2)
                square_sum(m, C - 1)

            def residual(slot, x, m, extra=None):
                for j in range(4):
                    features(slot + j, x)
                    if extra:
                        extra(j)
                    if j >= 1:
                        square_sum(m, 2 * j - 2)
                        square_sum(m, 2 * j - 1)
                square_sum(m, C - 2)
                square_sum(m, C - 1)

            def attention(n, score, value, out_banks):
                if n >= 1:
                    pe.wait_ge(S("probsT_copied"), n)
                for hd in range(4):
                    score(hd, 0, ps[:, 5, hd * P:(hd + 1) * P])
                for hd in range(4):
                    last = score(hd, 1, ps[:, 6 + hd // 2, (hd % 2) * T:(hd % 2 + 1) * T])
                last.then_inc(S("scores_ready"), 1)
                return lambda: values(n, value, out_banks)

            def values(n, value, probs):
                pe.wait_ge(S("probs_ready"), n + 1)
                for hd in range(4):
                    nc.tensor.transpose(ps[:, 5, hd * P:(hd + 1) * P], probs[:, hd * P:(hd + 1) * P], ident)
                for b in range(TB):
                    for hd in range(4):
                        at = 512 + hd * T + b * P
                        last = nc.tensor.transpose(ps[:, 6 + b, hd * P:(hd + 1) * P], probs[:, at:at + P], ident)
                last.then_inc(S("probsT_ready"), 1)
                pe.wait_ge(S("probsT_copied"), n + 1)
                if n >= 1:
                    pe.wait_ge(S("attended_read"), n)
                for hd in range(4):
                    last = value(hd)
                last.then_inc(S("attended"), 1)

            pe.wait_ge(S("constants"), 2)
            pe.wait_ge(S("vec_landed"), 32)
            for c in range(C):
                square_sum(0, c)

            features(S_FFN1, nrm, n_at=0)
            for j in range(1, RING):
                features(j, nrm)
            turns = (2 * FB - RING) // RING
            with pe.Fori(0, turns) as i:
                for j in range(RING):
                    features(RING + j, nrm, i * RING)
                    if j == 1:
                        modulation(0, i * RING)
            for j in range((turns + 1) * RING, 2 * FB):
                features(j, nrm)
            modulation(MODS - 2 * RING)
            down(S_DOWN1, 1, MODS - RING)

            def level(n, q, k):
                pe.wait_ge(S("level_operands"), n + 1)
                if n == 0:
                    pe.wait_ge(S("std_ready"), 2)
                else:
                    pe.wait_ge(S("level_read"), n)
                for hd in range(HH):
                    for b in range(TB):
                        at = slice(b * P, (b + 1) * P)
                        last = mm(ps[:, 4 + hd // 2, (hd % 2 * 2 + b) * P:(hd % 2 * 2 + b + 1) * P],
                                  k[:, hd, at], q[:, hd, at], start=True, stop=True)
                last.then_inc(S("level_ready"), 1)

            def latent(n):
                if 2 <= n <= 10:
                    pe.wait_ge(S("latent_copied"), n - 1)
                return ps[:, 6 + n % 2, :].rearrange("p (t n) -> p t n", t=2)

            def latent_sums():
                pe.wait_ge(S("latent_squared"), 2)
                to = latent(0)
                mm(to[:, 0, :], ones[:, :], csq[:, 0, :], start=True, stop=False)
                mm(to[:, 0, :], ones[:, :], csq[:, 1, :], start=False, stop=True)
                mm(to[:, 1, :], ones[:, :], csq[:, 2, :], start=True, stop=True).then_inc(S("latent_ready"), 1)

            def q_up(n):
                to = latent(n)
                width, off = (P, 0) if n < 3 else (ROPE, P)
                if n == 1:
                    pe.wait_ge(S("latent_normed"), 1)
                for j in range(2):
                    hd = (n - 1) % 2 * 2 + j
                    for k in range(2):
                        last = mm(to[0:width, j, :], w_q_up[:, k, hd * QK + off:hd * QK + off + width],
                                  cqn[:, k, :], start=(k == 0), stop=(k == 1))
                last.then_inc(S("latent_ready"), 1)

            def k_up(n):
                to = latent(n)
                if n == 5:
                    pe.wait_ge(S("latent_normed"), 2)
                for j in range(2):
                    last = mm(to[:, j, :], w_kv_up[:, (n - 5) * 2 + j, 0:P], cqn[:, 2, :], start=True, stop=True)
                last.then_inc(S("latent_ready"), 1)

            def v_up(n):
                to = latent(n)
                b = n - 7
                mm(to.rearrange("p t n -> p (t n)"), cqn[:, 2, b * P:(b + 1) * P], w_kv_up[:, :, P:2 * P],
                   start=True, stop=True).then_inc(S("latent_ready"), 1)

            def swapped(n):
                to = latent(n)
                j = (n - 9) * 2
                if n == 9:
                    pe.wait_ge(S("latent_copied"), 9)
                if n == 11:
                    pe.wait_ge(S("rotated"), 1)
                width = min(2, HH + 1 - j) * T
                mm(to.rearrange("p t n -> p (t n)")[0:ROPE, 0:width], K("swap", ROPE),
                   xr[0:ROPE, j:j + width // T, :], start=True, stop=True).then_inc(S("latent_ready"), 1)

            features(S_IN, nrm, n_at=C)
            features(S_IN + 1, nrm)
            features(S_IN + 2, nrm)
            features(S_IN + 3, nrm)
            features(S_IN + 4, nrm)
            level(0, hq, hk)
            features(S_IN + 5, nrm, tiles=((0, P), (P, ROPE)))
            level(1, hqf, hk)
            tokens(S_IN + 6, nrm)
            latent_sums()
            level(2, hqf, hk)
            tokens(S_IN + 7, nrm)
            for n in (1, 2, 3, 4):
                q_up(n)
            level(3, hqf, hk)
            features(S_IN + 8, nrm)
            k_up(5)
            k_up(6)
            level(4, hqf, hk)
            features(S_IN + 9, nrm)
            v_up(7)
            v_up(8)
            level(5, hqf, hk)
            swapped(9)
            swapped(10)
            level(6, hqf, hk)
            swapped(11)
            level(7, hqf, hk)
            pe.wait_ge(S("level_operands"), LEVELS + 2)
            pe.wait_ge(S("level_read"), LEVELS + 1)
            for hd in range(HH):
                last = mm(ps[:, 4, hd * P:(hd + 1) * P], hk[:, hd, 0:P], hqf[:, hd, P:T], start=True, stop=True)
            last.then_inc(S("level_ready"), 1)
            pe.wait_ge(S("scores_built"), 1)
            pe.wait_ge(S("rotated"), 3)
            for hd in range(HH):
                to = ps[:, 6 + hd // 2, (hd % 2) * T:(hd % 2 + 1) * T]
                cols = slice(hd * P, (hd + 1) * P)
                mm(to[:, 0:P], hv[:, 0, cols], scT[:, hd, 0, :], start=True, stop=True)
                mm(to[:, P:T], hv[:, 1, cols], scT[:, hd, 1, :], start=True, stop=False)
                last = mm(to[:, P:T], hv[:, 0, cols], sc7[:, hd, :], start=False, stop=True)
            last.then_inc(S("hg_out"), 1)
            pe.wait_ge(S("hg_squared"), 1)
            for j in range(2):
                last = mm(ps[:, 4 + j, :], ones[:, :], osq[:, 2 * j:2 * j + 2, :], start=True, stop=True)
            last.then_inc(S("hg_sums"), 1)
            pe.wait_ge(S("hg_std"), 1)
            pe.wait_ge(S("hg_copied"), 1)

            def mla_score(hd, b, to):
                at, upto = slice(b * P, (b + 1) * P), (b + 1) * P
                mm(to, qn[:, hd, at], kn[:, hd, 0:upto], start=True, stop=False)
                return mm(to, rot[0:ROPE, hd, at], rot[0:ROPE, HH, 0:upto], start=False, stop=True)

            def mla_value(hd):
                to = ps[:, 5 + hd // 2, (hd % 2) * T:(hd % 2 + 1) * T]
                pt = m["prT"]
                cols = slice(hd * P, (hd + 1) * P)
                mm(to[:, 0:P], va[:, 0, cols], pt[:, cols], start=True, stop=True)
                mm(to[:, P:T], va[:, 0, cols], pt[:, 512 + hd * P:512 + (hd + 1) * P], start=True, stop=False)
                return mm(to[:, P:T], va[:, 1, cols], pt[:, 1024 + hd * P:1024 + (hd + 1) * P], start=False, stop=True)

            pe.wait_ge(S("rope_done"), 1)
            attention(0, mla_score, mla_value, m["pr"])()

            pe.wait_ge(S("attended_read"), 1)
            pe.wait_ge(S("hg_gated"), 1)
            residual(S_OUT, mixed, 2)

            pe.wait_ge(S("normed"), 3 * C)
            turns = (2 * FB) // RING
            with pe.Fori(0, turns) as i:
                for j in range(RING):
                    features(S_FFN2 + j, nrm, i * RING)
            for j in range(turns * RING, 2 * FB):
                features(S_FFN2 + j, nrm)
            down(S_DOWN2, 3)

            def ple_product(j):
                if j == 0:
                    pe.wait_ge(S("p_landed"), 16)
                if j >= 2:
                    pe.wait_ge(S("ple_added"), j - 1)
                for t in range(2):
                    for k in range(2):
                        last = mm(ps[:, 5 + j % 2, t * T:(t + 1) * T], w_ple[:, k, (2 * j + t) * P:(2 * j + t + 1) * P],
                                  pT[:, k, :], start=(k == 0), stop=(k == 1))
                last.then_inc(S("ple_ready"), 1)

            pe.wait_ge(S("normed"), 4 * C)
            residual(S_PLE, nrm, 4, ple_product)
            for c in range(C):
                square_sum(5, c)

            pe.wait_ge(S("normed"), 5 * C)
            pe.wait_ge(S("std_ready"), 6)
            for k in range(C):
                last = mm(ps[0:96, 5, 0:T], wf[:, k, :], nrm[:, k, :], start=(k == 0), stop=(k == C - 1))
            last.then_inc(S("forget_ready"), 1)
            for base, step in ((S_IN2, features), (S_IN2 + 4, features), (S_IN2 + 8, tokens)):
                for j in range(4):
                    step(base + j, nrm)

            def fa_score(group):
                def score(hd, b, to):
                    head = 4 * group + hd
                    return mm(to, qp[:, head, b * P:(b + 1) * P], kp[:, head, 0:(b + 1) * P], start=True, stop=True)
                return score

            def fa_value(group):
                def value(hd):
                    head = 4 * group + hd
                    rows = slice((hd % 2) * AD, (hd % 2 + 1) * AD)
                    to = ps[rows, 4, (hd // 2) * T:(hd // 2 + 1) * T]
                    pt, cols = s["prT"], slice(head * AD, (head + 1) * AD)
                    mm(to[:, 0:P], v2[:, 0, cols], pt[:, hd * P:(hd + 1) * P], start=True, stop=True)
                    mm(to[:, P:T], v2[:, 0, cols], pt[:, 512 + hd * P:512 + (hd + 1) * P], start=True, stop=False)
                    return mm(to[:, P:T], v2[:, 1, cols], pt[:, 1024 + hd * P:1024 + (hd + 1) * P],
                              start=False, stop=True)
                return value

            pe.wait_ge(S("decay_rows"), 4)
            pe.wait_ge(S("banks_freed"), S_IN2 + 12)
            slot = S_IN2 + 12
            rest = attention(1, fa_score(0), fa_value(0), s["pr"])
            for group in range(4):
                for j in range(2):
                    features(slot, nrm)
                    slot += 1
                rest()
                if group < 3:
                    rest = attention(group + 2, fa_score(group + 1), fa_value(group + 1), s["pr"])
            features(slot, nrm)
            features(slot + 1, nrm)
            pe.wait_ge(S("pooled"), 1)
            pe.wait_ge(S("probsT_copied"), 5)
            for g in range(4):
                if g >= 2:
                    pe.wait_ge(S("pool_read"), g - 1)
                for t in range(2):
                    last = mm(ps[:, 5 + g % 2, t * T:(t + 1) * T], w_pool[:, g, t * P:(t + 1) * P], pooled[:, g, :],
                              start=True, stop=True)
                last.then_inc(S("pool_ready"), 1)
            pe.wait_ge(S("branches"), 1)
            residual(S_OUT2, gb, 6)

            pe.wait_ge(S("normed"), 6 * C)

            def key_scores(hd):
                r = (S_PQ + hd) % RING
                pe.wait_ge(S("queries_copied"), hd + 1)
                for b in range(TB):
                    for p in range(2):
                        last = mm(ps[:, r, (2 * b + p) * P:(2 * b + p + 1) * P], qT[:, hd % 2 * 2 + p, b * P:(b + 1) * P],
                                  keys[:, 2 * hd + p, :], start=True, stop=True)
                last.then_inc(S("key_scores"), 1)

            turned = 0
            def turn_around(src, n):
                nonlocal turned
                if turned >= 2:
                    pe.wait_ge(S("turned_copied"), turned - 1)
                b, half = n // 2, n % 2
                for c in range(4):
                    last = nc.tensor.transpose(ps[:, 5 + turned % 2, c * P:(c + 1) * P],
                                               src[:, half * 4 + c, b * P:(b + 1) * P], ident)
                last.then_inc(S("turned"), 1)
                turned += 1

            features(S_PQ, nrm)
            for n in range(4):
                turn_around(nrm, n)
            key_scores(0)
            for hd in range(1, PH):
                features(S_PQ + hd, nrm)
                if hd == 3:
                    pe.wait_ge(S("gate_columns"), 1)
                    for n in range(2):
                        if turned >= 2:
                            pe.wait_ge(S("turned_copied"), turned - 1)
                        for c in range(4):
                            last = nc.tensor.transpose(ps[:, 5 + turned % 2, c * P:(c + 1) * P],
                                                       gtb[:, n * 4 + c, :], ident)
                        last.then_inc(S("turned"), 1)
                        turned += 1
                key_scores(hd)
            pe.wait_ge(S("turned_copied"), 6)
            for b in range(4):
                mm(ps[:, 4 + b, :], zeros[:, :], keys[:, 0:4, :], start=True, stop=False, skip_group_check=True)

            def weigh(j, k, turn):
                acc = 4 + 2 * (j % TB)
                g = j * TK + k
                pe.wait_ge(S("diagonals"), turn * TK + (g + 1))
                pe.wait_ge(S(f"v_landed{g % RV}"), turn * (TK * 16 // RV) + 16 * (g // RV + 1))
                mm(ps[:, acc, :], diag[:, k, :], vbuf[:, g % RV, 0:512], start=False, stop=False,
                   skip_group_check=True)
                mm(ps[:, acc + 1, :], diag[:, k, :], vbuf[:, g % RV, 512:D], start=False, stop=False,
                   skip_group_check=True).then_inc(S("weighed"), 1)

            pe.wait_ge(S("banks_freed"), S_END)
            for b in range(TB):
                for c in range(C):
                    last = nc.tensor.transpose(ps[:, 2 * b + c // 4, (c % 4) * P:(c % 4 + 1) * P],
                                               h[:, c, b * P:(b + 1) * P], ident)
            last.then_inc(S("residual_turned"), 1)

            with pe.Fori(0, UNITS // UB) as i:
                for j in range(UB):
                    for k in range(TK):
                        weigh(j, k, i * UB)

        @block.scalar
        def _(act):
            fn = nc.scalar.activation
            own = Chain(act, S("act_own"), S("act_waited"))

            act.dma_start(h[:, :, :], a["x"]).then_inc(S("x_landed"), 16)
            act.dma_start(vec[:, :], a["vec"]).then_inc(S("vec_landed"), 16)
            act.dma_start(con[:, :], a["con"]).then_inc(S("vec_landed"), 16)
            act.dma_start(posi[:, :], a["pos"].partition_broadcast(ROPE).rearrange("p a t -> p (a t)")
                          ).then_inc(S("pos_landed"), 16)
            act.dma_start(wf[:, :, :], a["wf"]).then_inc(S("small_landed"), 16)
            act.dma_start(small[:, :], a["small"]).then_inc(S("small_landed"), 16)
            act.dma_start(lev_mask[:, :, :], a["lev_mask"]).then_inc(S("small_landed"), 16)
            act.dma_start(inv_count[:, :, :].rearrange("p g t -> p (g t)"),
                          a["inv_count"].partition_broadcast(P).rearrange("p a t -> p (a t)")
                          ).then_inc(S("small_landed"), 16)
            act.dma_start(keys[:, :, :], a["keys"]).then_inc(S("small_landed"), 16)
            act.dma_start(pT[:, :, :], a["p"]).then_inc(S("p_landed"), 16)

            def square(m, c):
                if m == 0:
                    act.wait_ge(S("x_landed"), 16)
                elif m == 5:
                    act.wait_ge(S("block1_out"), c + 1)
                elif m in (1, 3):
                    act.wait_ge(S("banks_freed"), {1: S_DOWN1, 3: S_DOWN2}[m] + c + 1)
                else:
                    act.wait_ge(S("banks_freed"), {2: S_OUT, 4: S_PLE, 6: S_OUT2}[m] + c // 2 + 1)
                if m:
                    act.wait_ge(S("sum_ready"), m)
                fn(sq[:, c, :], h[:, c, :], ACT.Square).then_inc(S("squared"), 1)

            def root(m):
                act.wait_ge(S("sum_ready"), m + 1)
                fn(std[:, 0, :], ps[:, 4, 0:T], ACT.Sqrt, bias=eps[:, 0:1], scale=1.0 / D).then_inc(S("std_ready"), 1)

            def shift(m, first):
                for c in range(C):
                    act.wait_ge(S("scaled"), (m - 5) * C + c + 1)
                    fn(nrm[:, c, :], nrm[:, c, :], ACT.Identity, bias=mod[:, first + c:first + c + 1]
                       ).then_inc(S("normed"), 1)

            act.wait_ge(S("constants"), 2)
            for c in range(C):
                square(0, c)
            act.wait_ge(S("lb_shifted"), 1)
            fn(lb[:, 2:4, :], lb[:, 0:2, :], ACT.Exp).then_inc(S("lb_exp"), 1)
            act.wait_ge(S("angle"), 1)
            own(fn(sin[:, :], ang[:, 0, :], ACT.Sin))
            fn(cos[:, :], ang[:, 0, :], ACT.Sin, scale=0.5).then_inc(S("sines"), 1)
            root(0)

            def gate(slot, width, turn=0, first=False):
                act.wait_ge(S("slots_done"), turn + (slot + 1))
                if not first:
                    act.wait_ge(S("banks_freed"), turn + (slot - width + 2))
                fn(silu[:, :, :], pair(slot % RING), ACT.Silu).then_inc(S("silu_ready"), 1)

            gate(0, 2, first=True)
            with act.Fori(0, FB // 2) as i:
                gate(2, 2, i * 4)
                gate(4, 2, i * 4)
            for c in range(C):
                square(1, c)
            root(1)

            def copied(slot, *ins):
                ins[-1].then_inc(S("banks_freed"), 1)

            act.wait_ge(S("banks_freed"), S_IN)
            for j in range(2):
                act.wait_ge(S("slots_done"), S_IN + j + 1)
                fn(heads(m["b1"], HH)[:, 2 * j:2 * j + 2, :], pair((S_IN + j) % RING), ACT.Sigmoid)
                copied(S_IN + j, fn(hk[:, 2 * j:2 * j + 2, :], pair((S_IN + j) % RING), ACT.Sigmoid, scale=-1.0))
            for j in range(2):
                act.wait_ge(S("slots_done"), S_IN + j + 3)
                copied(S_IN + 2 + j, fn(hq[:, 2 * j:2 * j + 2, :], pair((S_IN + 2 + j) % RING), ACT.Copy))
            act.wait_ge(S("slots_done"), S_IN + 5)
            copied(S_IN + 4, fn(cq[:, 0:2, :], pair((S_IN + 4) % RING), ACT.Copy))
            act.wait_ge(S("banks_freed"), S_IN + 5)
            fn(csq[:, 0:2, :], cq[:, 0:2, :], ACT.Square).then_inc(S("latent_squared"), 1)
            act.wait_ge(S("slots_done"), S_IN + 6)
            own(fn(cq[:, 2, :], pair((S_IN + 5) % RING)[:, 0, :], ACT.Copy))
            copied(S_IN + 5, fn(xr[0:ROPE, HH, :], pair((S_IN + 5) % RING)[0:ROPE, 1, :], ACT.Copy))
            fn(csq[:, 2, :], cq[:, 2, :], ACT.Square).then_inc(S("latent_squared"), 1)

            def values_out(j):
                act.wait_ge(S("slots_done"), S_IN + 7 + j)
                copied(S_IN + 6 + j, fn(hv[:, :, j * T:(j + 1) * T], pair((S_IN + 6 + j) % RING), ACT.Copy))

            def latent_out(n, to, rows=P):
                act.wait_ge(S("latent_ready"), n + 1)
                src = ps[0:rows, 6 + n % 2, :]
                fn(to, src if len(to.shape) == 2 else src.rearrange("p (t n) -> p t n", t=2), ACT.Copy
                   ).then_inc(S("latent_copied"), 1)

            values_out(0)
            act.wait_ge(S("latent_ready"), 1)
            own(fn(std[:, 0, :], ps[:, 6, 0:T], ACT.Sqrt, bias=eps[:, 0:1], scale=1.0 / (2 * P)))
            fn(std[:, 1, :], ps[:, 6, T:2 * T], ACT.Sqrt, bias=eps[:, 0:1], scale=1.0 / P).then_inc(S("latent_copied"), 1)
            values_out(1)
            latent_out(1, qn[:, 0:2, :])
            latent_out(2, qn[:, 2:4, :])
            latent_out(3, xr[0:ROPE, 0:2, :], ROPE)
            latent_out(4, xr[0:ROPE, 2:4, :], ROPE)

            def out_gate(j):
                act.wait_ge(S("slots_done"), S_IN + 9 + j)
                copied(S_IN + 8 + j, fn(hg[:, 2 * j:2 * j + 2, :], pair((S_IN + 8 + j) % RING), ACT.Silu))

            out_gate(0)
            latent_out(5, kn[:, 0:2, :])
            latent_out(6, kn[:, 2:4, :])
            out_gate(1)
            latent_out(7, va[:, 0, :])
            latent_out(8, va[:, 1, :])
            act.wait_ge(S("hg_copied"), 1)
            fn(osq[:, :, :], ho[:, :, :], ACT.Square
               ).then_inc(S("hg_squared"), 1)
            act.wait_ge(S("hg_sums"), 1)
            fn(ostd[:, :, :].rearrange("p h t -> p (h t)"), ps[:, 4:6, :].rearrange("p b n -> p (b n)"), ACT.Sqrt,
               bias=eps[:, 0:1], scale=1.0 / P).then_inc(S("hg_std"), 1)

            def exponentials(n, pr):
                act.wait_ge(S("logits"), n + 1)
                fn(pr, pr, ACT.Exp).then_inc(S("probs_exp"), 1)

            def turned_probs(n, prT):
                act.wait_ge(S("probsT_ready"), n + 1)
                if n >= 1:
                    act.wait_ge(S("attended"), n)
                fn(prT, ps[:, 5:8, :].rearrange("p b n -> p (b n)"), ACT.Copy).then_inc(S("probsT_copied"), 1)

            exponentials(0, m["pr"])
            turned_probs(0, m["prT"])
            for c in range(C):
                square(2, c)
            root(2)

            with act.Fori(0, FB // 2) as i:
                gate(S_FFN2, 2, i * 4)
                gate(S_FFN2 + 2, 2, i * 4)
            gate(S_FFN2 + 2 * (FB - 1), 2)
            for c in range(C):
                square(3, c)
            root(3)

            for j in range(4):
                act.wait_ge(S("slots_done"), S_PLE + j + 1)
                if j:
                    act.wait_ge(S("banks_freed"), S_PLE + j)
                fn(silu[:, :, :], pair((S_PLE + j) % RING), ACT.Sigmoid).then_inc(S("ple_gate"), 1)
                if j:
                    square(4, 2 * j - 2)
                    square(4, 2 * j - 1)
            square(4, C - 2)
            square(4, C - 1)
            root(4)
            for c in range(C):
                square(5, c)
            root(5)
            shift(5, 0)

            act.wait_ge(S("decay_abs"), 1)
            own(fn(fl[0:96, 1, :], fl[0:96, 1, :], ACT.Exp))
            fn(fl[0:96, 1, :], fl[0:96, 1, :], ACT.Ln, bias=1.0).then_inc(S("decay_log"), 1)

            act.wait_ge(S("padded"), 1)
            act.wait_ge(S("banks_freed"), S_IN2)
            for dst, base in ((qp, S_IN2), (kp, S_IN2 + 4)):
                for j in range(4):
                    act.wait_ge(S("slots_done"), base + j + 1)
                    src = pair((base + j) % RING)
                    fn(dst[0:AD, 4 * j:4 * j + 4:2, :], src[0:AD, :, :], ACT.Copy)
                    copied(base + j, fn(dst[AD:P, 4 * j + 1:4 * j + 4:2, :], src[AD:P, :, :], ACT.Copy))
            for j in range(4):
                act.wait_ge(S("slots_done"), S_IN2 + 8 + j + 1)
                copied(S_IN2 + 8 + j, fn(v2[:, :, j * T:(j + 1) * T], pair((S_IN2 + 8 + j) % RING), ACT.Copy))

            def in2_out(j):
                slot = S_IN2 + 12 + j
                act.wait_ge(S("slots_done"), slot + 1)
                if j < 2:
                    copied(slot, fn(up[:, 2 * j:2 * j + 2, 16:16 + T], pair(slot % RING), ACT.Copy))
                else:
                    to = ga if j < 6 else gb
                    c = (j - 2) % 4 * 2
                    copied(slot, fn(to[:, c:c + 2, :], pair(slot % RING), ACT.Sigmoid))

            for group in range(4):
                exponentials(group + 1, s["pr"])
                in2_out(2 * group)
                in2_out(2 * group + 1)
                turned_probs(group + 1, s["prT"])
            in2_out(8)
            in2_out(9)
            for c in range(C):
                square(6, c)
            root(6)
            shift(6, 3 * C)

            act.dma_start(fgrow, a["final_g"].partition_broadcast(P).rearrange("p a t -> p (a t)")
                          ).then_inc(S("final_landed"), 16)
            turned = 0

            def turned_out(to):
                nonlocal turned
                act.wait_ge(S("turned"), turned + 1)
                fn(to, ps[:, 5 + turned % 2, :], ACT.Copy).then_inc(S("turned_copied"), 1)
                turned += 1

            for hd in range(PH):
                r = (S_PQ + hd) % RING
                act.wait_ge(S("slots_done"), S_PQ + hd + 1)
                if hd == 0:
                    act.wait_ge(S("banks_freed"), S_PQ)
                if hd >= 2:
                    act.wait_ge(S("key_scores"), hd - 1)
                fn(qT[:, hd % 2 * 2:hd % 2 * 2 + 2, :], pair(r), ACT.Copy).then_inc(S("queries_copied"), 1)
                for n in range(4):
                    if hd == 0:
                        turned_out(h2[:, n // 2, (n % 2) * 512:(n % 2 + 1) * 512])
                    if hd == 3 and n < 2:
                        turned_out(gtrow[:, n * 512:(n + 1) * 512])
                act.wait_ge(S("key_scores"), hd + 1)
                fn(scores[:, hd, :, :].rearrange("p b n -> p (b n)"), ps[:, r, :], ACT.Copy
                   ).then_inc(S("banks_freed"), 1)

            def weights(q):
                few = e["few"][:, q * 96:(q + 1) * 96]
                return {"expo": few[:, 0:16], "total": few[:, 16:17], "less": few[:, 17:18],
                        "inv": few[:, 18:19], "dots": few[:, 32:48], "act": few[:, 48:64], "w": few[:, 64:80]}

            def gate_exp(j, turn=0):
                q = j % UB
                act.wait_ge(S("chosen"), turn + (j + 1))
                top = e["vals"][:, q * 64 + 32:q * 64 + 48]
                fn(weights(q)["expo"], top, ACT.Exp, bias=weights(q)["less"], accum_out=weights(q)["total"]
                   ).then_inc(S("gates_exp"), 1)

            def activate(j, turn=0):
                w = weights(j)
                act.wait_ge(S("dotted"), turn * TK + (j + 1) * TK)
                fn(w["act"], w["dots"], ACT.Gelu).then_inc(S("gelu_ready"), 1)
                act.wait_ge(S("weights"), turn + (j + 1))
                for k in range(TK):
                    g = j * TK + k
                    if not isinstance(turn, int) or turn or g >= TK:
                        act.wait_ge(S("weighed"), turn * TK + (g - TK + 1))
                    fn(diag[:, k, :], ident, ACT.Copy, scale=w["w"][:, k:k + 1]).then_inc(S("diagonals"), 1)

            for j in range(AHEAD):
                gate_exp(j)

            def expert_turn(turn, last):
                for j in range(UB):
                    activate(j, turn)
                    if not last or j + AHEAD < UB:
                        gate_exp(j + AHEAD, turn)

            expert_turn(0, False)
            with act.Fori(1, UNITS // UB - 1) as i:
                expert_turn(i * UB, False)
            expert_turn(UNITS - UB, True)

            for b in range(TB):
                act.wait_ge(S("summed"), b + 1)
                own(fn(ubuf[:, 2 + b, :], ubuf[:, b, :], ACT.Square, accum_out=lb[:, 4 + b, 0:1]))
                fn(lb[:, 6 + b, 0:1], lb[:, 4 + b, 0:1], ACT.Sqrt, bias=eps[:, 0:1], scale=1.0 / D
                   ).then_inc(S("last_std"), 1)

        @block.vector
        def _(dve):
            v = nc.vector
            own = Chain(dve, S("dve_own"), S("dve_waited"))

            def cols(ap, n):
                return ap.unsqueeze(2).to_broadcast([ap.shape[0], ap.shape[1], n])

            def over(ap, n):
                return ap.unsqueeze(1).to_broadcast([ap.shape[0], n, ap.shape[1]])

            def inverse_std(m):
                dve.wait_ge(S("std_ready"), m + 1)
                own(v.reciprocal(rstd[:, 0, :], std[:, 0, :]))

            def norm(m, gain, to, sem):
                inverse_std(m)
                for c in range(C):
                    v.scalar_tensor_tensor(to[:, c, :], h[:, c, :], gain[:, c:c + 1], rstd[:, 0, :], ALU.mult,
                                           ALU.mult).then_inc(S(sem), 1)

            dve.wait_ge(S("vec_landed"), 32)
            rows = V("lb", 0, 2 * HH).rearrange("p (r h) -> p r h", r=2)
            own(v.tensor_tensor(lb[:, 4, :], rows[:, 0, :], rows[:, 1, :], ALU.max))
            v.tensor_tensor(lb[:, 0:2, :], rows, over(lb[:, 4, :], 2), ALU.subtract).then_inc(S("lb_shifted"), 1)
            dve.wait_ge(S("pos_landed"), 16)
            own(v.tensor_copy(ang[:, 1, :], posi[:, :]))
            own(v.tensor_scalar(ang[:, 0, :], ang[:, 1, :], K("inv_freq", ROPE), None, ALU.mult))
            own(v.tensor_scalar(ang[:, 1, :], ang[:, 0, :], TURN_INV, None, ALU.mult))
            own(v.tensor_scalar(ang[:, 2, :], ang[:, 1, :], ROUND, None, ALU.add))
            own(v.tensor_scalar(ang[:, 1, :], ang[:, 2, :], ROUND, None, ALU.subtract))
            for part in TURN:
                own(v.scalar_tensor_tensor(ang[:, 0, :], ang[:, 1, :], -part, ang[:, 0, :], ALU.mult, ALU.add))
            v.tensor_scalar(ang[:, 0, :], ang[:, 0, :], HALF_TURN, -HALF_TURN, ALU.min, ALU.max).then_inc(S("angle"), 1)
            norm(0, V("ffn1", 0, C), nrm, "normed")
            dve.wait_ge(S("sines"), 1)
            own(v.tensor_tensor(ang[:, 2, :], cos[:, :], cos[:, :], ALU.mult))
            own(v.tensor_scalar(cos[:, :], ang[:, 2, :], -2.0, 1.0, ALU.mult, ALU.add))
            dve.wait_ge(S("lb_exp"), 1)
            own(v.tensor_tensor(lb[:, 4, :], lb[:, 2, :], lb[:, 3, :], ALU.add))
            own(v.reciprocal(lb[:, 5, :], lb[:, 4, :]))
            own(v.tensor_tensor(lb[:, 0, :], lb[:, 2, :], lb[:, 5, :], ALU.mult))
            own(v.tensor_scalar(lb[:, 1, :], lb[:, 0, :], -1.0, 1.0, ALU.mult, ALU.add))

            def gated(slot, b, silus, turn=0):
                dve.wait_ge(S("slots_done"), turn + (slot + 2))
                dve.wait_ge(S("silu_ready"), silus)
                v.tensor_tensor(gu[:, b, :] if isinstance(b, slice) else gu[:, bass.ds(b, 2), :], silu[:, :, :],
                                pair((slot + 1) % RING), ALU.mult).then_inc(S("banks_freed"), 2)

            def weighted(j, turn=0, first=False):
                r, to = j % MOD_RING, mod_sum[:, j % RING, :]
                if j % RING == 0 and not first:
                    dve.wait_ge(S("mod_read"), mod_turn + j // RING)
                landed = 16 * (j // MOD_RING + 1)
                dve.wait_ge(S(f"mod_landed{r}"), turn * (16 // MOD_RING) + landed)
                own(v.tensor_scalar(to, wm[:, r, 0, :], V("c", 0), None, ALU.mult))
                for k in range(1, C):
                    own(v.scalar_tensor_tensor(to, wm[:, r, k, :], V("c", k), to, ALU.mult, ALU.add))
                dve.sem_inc(S("mod_summed"), 1)

            gated(0, slice(0, 2), 1)
            for j in range(RING):
                weighted(j, first=True)
            with dve.Fori(0, FB // 2) as i:
                mod_turn = i
                own.loop(i, RING * C)
                gated(2, i * 4 + 2, i * 2 + 2, i * 4)
                weighted(RING, i * RING)
                weighted(RING + 1, i * RING)
                gated(4, i * 4 + 4, i * 2 + 3, i * 4)
                weighted(RING + 2, i * RING)
                weighted(RING + 3, i * RING)
            own.end(FB // 2)

            def half_residual(slot):
                for j in range(C):
                    dve.wait_ge(S("slots_done"), slot + j + 1)
                    v.scalar_tensor_tensor(h[:, j, :], ps[:, (slot + j) % RING, 0:T], 0.5, h[:, j, :], ALU.mult,
                                           ALU.add).then_inc(S("banks_freed"), 1)

            half_residual(S_DOWN1)
            norm(1, V("mix", 0, C), nrm, "normed")
            dve.wait_ge(S("mod_read"), MODS // RING)
            own(v.tensor_tensor(mod[:, :], ps[:, 5, 0:2 * MODS], V("b_mod", 0, 2 * MODS), ALU.add))

            f = heads(m["b0"], HH)
            raw = heads(m["b1"], HH)
            for hd in range(HH):
                if hd % 2 == 0:
                    dve.wait_ge(S("banks_freed"), S_IN + hd // 2 + 1)
                one_less, low = lb[:, 1, hd:hd + 1], lb[:, 0, hd:hd + 1]
                v.tensor_scalar(f[:, hd, :], raw[:, hd, :], one_less, low, ALU.mult, ALU.add)
                own(v.tensor_scalar(hk[:, hd, :], hk[:, hd, :], one_less, None, ALU.mult))
            dve.wait_ge(S("banks_freed"), S_IN + 4)
            v.tensor_tensor(m["qf"], m["q"], m["b0"], ALU.mult).then_inc(S("level_operands"), 2)
            dve.wait_ge(S("small_landed"), 16 * 5)
            dve.wait_ge(S("scores_zeroed"), 1)

            def level_read(n):
                dve.wait_ge(S("level_ready"), n + 1)
                v.copy_predicated(m["sc"].rearrange("p (x t) -> p x t", x=2 * HH),
                                  over(lev_mask[:, n, :], 2 * HH),
                                  ps[:, 4:6, :].rearrange("p b n -> p (b n)").rearrange("p (x t) -> p x t", x=2 * HH)
                                  ).then_inc(S("level_read"), 1)

            def widen(n):
                z = 2 ** n
                src, dst = m[f"b{n % 2}"], m[f"b{(n + 1) % 2}"]
                blocks = HH * T // z
                whole = src[:, 0:blocks].rearrange("p (n two) -> p n two", two=2)
                qv = m["qf"].rearrange("p (n two z) -> p n two z", two=2, z=z)
                kv = m["k"].rearrange("p (n two z) -> p n two z", two=2, z=z)
                own(v.tensor_tensor(dst[:, 0:blocks // 2], whole[:, :, 0], whole[:, :, 1], ALU.mult))
                v.tensor_tensor(qv[:, :, 1, :], qv[:, :, 1, :], cols(whole[:, :, 0], z), ALU.mult)
                own(v.tensor_tensor(kv[:, :, 0, :], kv[:, :, 0, :], cols(whole[:, :, 1], z), ALU.mult))
                dve.sem_inc(S("level_operands"), 1)

            level_read(0)
            level_read(1)
            widen(0)

            def latent_inverse():
                dve.wait_ge(S("latent_copied"), 1)
                own(v.reciprocal(rstd[:, :, :].rearrange("p a t -> p (a t)"), std[:, :, :].rearrange("p a t -> p (a t)")))
                for k in range(2):
                    last = v.scalar_tensor_tensor(cqn[:, k, :], cq[:, k, :], V("q_a", k), rstd[:, 0, :], ALU.mult, ALU.mult)
                last.then_inc(S("latent_normed"), 1)
                v.scalar_tensor_tensor(cqn[:, 2, :], cq[:, 2, :], V("kv_a"), rstd[:, 1, :], ALU.mult, ALU.mult
                                       ).then_inc(S("latent_normed"), 1)

            latent_inverse()
            for n in range(2, LEVELS + 1):
                level_read(n)
                widen(n - 1)
                if n == 4:
                    dve.wait_ge(S("latent_copied"), 5)
                    v.tensor_tensor(rt[0:ROPE, :, :], xr[0:ROPE, :, :], over(cos[:, :], HH + 1), ALU.mult)
                if n >= 5:
                    j = (n - 5) * 2
                    k = min(2, HH + 1 - j)
                    dve.wait_ge(S("latent_ready"), 10 + n - 5)
                    own(v.tensor_tensor(rot[0:ROPE, j:j + k, :],
                                        ps[0:ROPE, 6 + (n - 5 + 9) % 2, 0:k * T].rearrange("p (t n) -> p t n", t=k),
                                        over(sin[:, :], k), ALU.mult))
                    dve.sem_inc(S("rotated"), 1)
            dve.wait_ge(S("level_ready"), LEVELS + 2)
            v.tensor_copy(m["sc7"], ps[:, 4, :]).then_inc(S("scores_built"), 1)
            v.tensor_tensor(rot[0:ROPE, :, :], rot[0:ROPE, :, :], rt[0:ROPE, :, :], ALU.add).then_inc(S("rope_done"), 1)

            dve.wait_ge(S("hg_out"), 1)
            own(v.tensor_copy(m["o"], ps[:, 6:8, :].rearrange("p b n -> p (b n)")))
            dve.sem_inc(S("hg_copied"), 1)
            dve.wait_ge(S("hg_std"), 1)
            own(v.reciprocal(osq, ostd))
            for hd in range(HH):
                own(v.scalar_tensor_tensor(ho[:, hd, :], ho[:, hd, :], V("hg_norm", hd), osq[:, hd, :], ALU.mult, ALU.mult))
            v.tensor_tensor(mixed[:, 0:HH, :], ho[:, :, :], hg[:, :, :], ALU.mult).then_inc(S("hg_gated"), 1)

            causal = K("causal")

            def softmax(n, pr, st, scale):
                p0 = pr[:, 0:512].rearrange("p (h t) -> p h t", h=4)
                p1 = pr[:, 512:1536].rearrange("p (h t) -> p h t", h=4)
                dve.wait_ge(S("scores_ready"), n + 1)
                if n >= 2:
                    dve.wait_ge(S("probsT_ready"), n)
                v.scalar_tensor_tensor(p0, ps[:, 5, :].rearrange("p (h t) -> p h t", h=4), scale,
                                       over(causal[:, P:2 * P], 4), ALU.mult, ALU.add)
                own(v.scalar_tensor_tensor(p1, ps[:, 6:8, :].rearrange("p b n -> p (b n)").rearrange(
                    "p (h t) -> p h t", h=4), scale, over(causal, 4), ALU.mult, ALU.add))
                v.tensor_reduce(st[:, 0:4], p0, AX, ALU.max)
                own(v.tensor_reduce(st[:, 4:8], p1, AX, ALU.max))
                v.tensor_tensor(p0, p0, cols(st[:, 0:4], P), ALU.subtract)
                own(v.tensor_tensor(p1, p1, cols(st[:, 4:8], T), ALU.subtract))
                dve.sem_inc(S("logits"), 1)

            def normalise(n, pr, st):
                p0 = pr[:, 0:512].rearrange("p (h t) -> p h t", h=4)
                p1 = pr[:, 512:1536].rearrange("p (h t) -> p h t", h=4)
                dve.wait_ge(S("probs_exp"), n + 1)
                v.tensor_reduce(st[:, 8:12], p0, AX, ALU.add)
                own(v.tensor_reduce(st[:, 12:16], p1, AX, ALU.add))
                own(v.reciprocal(st[:, 16:24], st[:, 8:16]))
                v.tensor_tensor(p0, p0, cols(st[:, 16:20], P), ALU.mult)
                own(v.tensor_tensor(p1, p1, cols(st[:, 20:24], T), ALU.mult))
                dve.sem_inc(S("probs_ready"), 1)

            softmax(0, m["pr"], m["st"], float(QK) ** -0.5)
            normalise(0, m["pr"], m["st"])
            dve.wait_ge(S("attended"), 1)
            v.tensor_copy(mixed[:, HH:C, :].rearrange("p h t -> p (h t)"), ps[:, 5:7, :].rearrange("p b n -> p (b n)")
                          ).then_inc(S("attended_read"), 1)

            dve.wait_ge(S("banks_freed"), S_OUT)
            for j in range(4):
                dve.wait_ge(S("slots_done"), S_OUT + j + 1)
                v.tensor_tensor(h[:, 2 * j:2 * j + 2, :], pair((S_OUT + j) % RING), h[:, 2 * j:2 * j + 2, :], ALU.add
                                ).then_inc(S("banks_freed"), 1)
            norm(2, V("ffn2", 0, C), nrm, "normed")

            with dve.Fori(0, FB // 2) as i:
                gated(S_FFN2, i * 4, i * 2 + (FB + 1), i * 4)
                gated(S_FFN2 + 2, i * 4 + 2, i * 2 + (FB + 2), i * 4)
            gated(S_FFN2 + 2 * (FB - 1), slice(2 * FB - 2, 2 * FB), 2 * FB)
            half_residual(S_DOWN2)
            norm(3, V("ple", 0, C), nrm, "normed")

            for j in range(4):
                dve.wait_ge(S("ple_gate"), j + 1)
                dve.wait_ge(S("ple_ready"), j + 1)
                own(v.tensor_tensor(silu[:, :, :], silu[:, :, :], ps[:, 5 + j % 2, :].rearrange("p (t n) -> p t n", t=2),
                                    ALU.mult))
                v.tensor_tensor(h[:, 2 * j:2 * j + 2, :], silu[:, :, :], h[:, 2 * j:2 * j + 2, :], ALU.add
                                ).then_inc(S("banks_freed"), 1)
                dve.sem_inc(S("ple_added"), 1)
            norm(4, V("final1", 0, C), h, "block1_out")

            def modulated_norm(m, gain, scale_at):
                co = coef[:, 0:C]
                own(v.tensor_scalar(coef[:, C:2 * C], mod[:, scale_at:scale_at + C], 1.0, None, ALU.add))
                own(v.tensor_tensor(co, coef[:, C:2 * C], gain, ALU.mult))
                norm(m, co, nrm, "scaled")

            modulated_norm(5, V("norm1", 0, C), C)

            dve.wait_ge(S("forget_ready"), 1)
            own(v.tensor_scalar(fl[0:96, 0, :], ps[0:96, 5, 0:T], vec[0:96, slice(*VEC["b_f"])], None, ALU.add))
            own(v.tensor_scalar(fl[0:96, 2, :], fl[0:96, 0, :], -1.0, None, ALU.mult))
            v.tensor_tensor(fl[0:96, 1, :], fl[0:96, 0, :], fl[0:96, 2, :], ALU.min).then_inc(S("decay_abs"), 1)
            dve.wait_ge(S("decay_abs"), 1)
            own(v.tensor_scalar(fl[0:96, 2, :], fl[0:96, 0, :], 0.0, None, ALU.min))
            own(v.memset(fl[0:96, 3, :], 1.0))
            dve.wait_ge(S("decay_log"), 1)
            own(v.tensor_tensor(fl[0:96, 0, :], fl[0:96, 2, :], fl[0:96, 1, :], ALU.subtract))
            own(v.tensor_tensor_scan(fl[0:96, 4, :], fl[0:96, 3, :], fl[0:96, 0, :], 0.0, ALU.mult, ALU.add))
            unscale = float(AD) ** 0.5
            own(v.tensor_scalar(fl[0:96, 0, :], fl[0:96, 4, :], K("is_value", 96), unscale, ALU.mult, ALU.mult))
            own(v.tensor_scalar(fl[0:96, 1, :], fl[0:96, 4, :], K("not_value", 96), -unscale, ALU.mult, ALU.mult))
            dve.wait_ge(S("padded"), 1)
            for row, odd in ((AD, 0), (0, 1)):
                rs = slice(row, row + 32)
                for dst, src, sel in ((qp, 0, "sel_q"), (kp, 1, "sel_k")):
                    v.tensor_tensor(dst[rs, odd:AH:2, :], over(fl[rs, src, :], AH // 2),
                                    cols(con[rs, CON[sel][0] + odd:CON[sel][1]:2], T), ALU.add
                                    ).then_inc(S("decay_rows"), 1)

            for group in range(4):
                n = group + 1
                softmax(n, s["pr"], s["st"], float(AD) ** -0.5)
                normalise(n, s["pr"], s["st"])
                dve.wait_ge(S("attended"), n + 1)
                v.tensor_copy(o2[:, 2 * group:2 * group + 2, :].rearrange("p c t -> p (c t)"), ps[:, 4, :]
                              ).then_inc(S("attended_read"), 1)

            dve.wait_ge(S("banks_freed"), S_OUT2)
            for c in range(C):
                g, t = c // 2, c % 2
                if t == 0:
                    dve.wait_ge(S("pool_ready"), g + 1)
                ins = v.scalar_tensor_tensor(ga[:, c, :], ps[:, 5 + g % 2, t * T:(t + 1) * T], V("pool_scale", c),
                                             ga[:, c, :], ALU.mult, ALU.mult)
                if t == 1:
                    ins.then_inc(S("pool_read"), 1)
            dve.wait_ge(S("attended_read"), 5)
            own(v.tensor_tensor(gb[:, :, :], gb[:, :, :], o2[:, :, :], ALU.mult))
            dve.wait_ge(S("pool_read"), 4)
            v.tensor_tensor(gb[:, :, :], gb[:, :, :], ga[:, :, :], ALU.add).then_inc(S("branches"), 1)

            for j in range(4):
                dve.wait_ge(S("slots_done"), S_OUT2 + j + 1)
                for t in range(2):
                    c = 2 * j + t
                    ins = v.scalar_tensor_tensor(h[:, c, :], pair((S_OUT2 + j) % RING)[:, t, :],
                                                 mod[:, 2 * C + c:2 * C + c + 1], h[:, c, :], ALU.mult, ALU.add)
                ins.then_inc(S("banks_freed"), 1)
            modulated_norm(6, V("norm2", 0, C), 4 * C)
            v.tensor_tensor(gtb, cols(mod[:, 5 * C:6 * C], P),
                            ones[:, :].unsqueeze(1).to_broadcast([P, C, P]), ALU.mult).then_inc(S("gate_columns"), 1)

            iota = K("iota")

            def top16(values, to_values, to_index, work):
                own(v.max(to_values[:, 0:8], values), apart=True)
                v.max_index(to_index[:, 0:8], to_values[:, 0:8], values)
                own(v.match_replace(work, to_values[:, 0:8], values, NEG), apart=True)
                own(v.max(to_values[:, 8:16], work), apart=True)
                own(v.max_index(to_index[:, 8:16], to_values[:, 8:16], work), apart=True)

            def choose(j, head, turn=0):
                q, b = j % UB, j % TB
                vals = e["vals"][:, q * 64:(q + 1) * 64]
                few = e["few"][:, q * 96:(q + 1) * 96]
                work, index = e["wk"], e["sel"].bitcast(U32)
                dve.wait_ge(S("banks_freed"), head + (S_PQ + 1))
                src = scores[:, head, b, :] if isinstance(head, int) else \
                    scores[:, bass.ds(head, 1), b, :].rearrange("p a n -> p (a n)")
                own(v.tensor_copy(work[:, 0:256], src), apart=True)
                for p in range(2):
                    top16(work[:, p * NK:(p + 1) * NK], vals[:, p * 16:(p + 1) * 16], index[:, p * 16:(p + 1) * 16],
                          work[:, 256:256 + NK])
                own(v.tensor_copy(work[:, 512:544], index))
                cand = work[:, 0:256]
                own(v.tensor_tensor(cand.rearrange("p (i j) -> p i j", i=TK), cols(vals[:, 0:TK], TK),
                                    over(vals[:, TK:2 * TK], TK), ALU.add), apart=True)
                top16(cand, vals[:, 32:48], index[:, 0:16], work[:, 256:512])
                own(v.tensor_scalar(few[:, 17:18], vals[:, 32:33], -1.0, None, ALU.mult))
                dve.sem_inc(S("chosen"), 1)
                own(v.tensor_scalar(index[:, 16:32], index[:, 0:16], TK - 1, None, ALU.bitwise_and))
                own(v.tensor_scalar(index[:, 0:16], index[:, 0:16], 4, None, ALU.logical_shift_right))
                own(v.tensor_copy(work[:, 544:576], index))
                hot = e["oh"].rearrange("p (k j) -> p k j", j=TK)
                own(v.tensor_tensor(hot, cols(work[:, 544:576], TK), over(iota, 2 * TK), ALU.is_equal))
                hot4 = e["oh"].rearrange("p (s k j) -> p s k j", s=2, j=TK)
                lists = work[:, 512:544].rearrange("p (s j) -> p s j", s=2).unsqueeze(2).to_broadcast([P, 2, TK, TK])
                own(v.tensor_tensor(hot4, hot4, lists, ALU.mult))
                own(v.tensor_reduce(work[:, 576:608], hot, AX, ALU.add))
                if j >= UB or not isinstance(turn, int):
                    dve.wait_ge(S("weighed"), turn * TK + (j - UB + 1) * TK)
                v.scalar_tensor_tensor(few[:, 80:96].bitcast(U32), work[:, 576:592], float(NK), work[:, 592:608],
                                       ALU.mult, ALU.add).then_inc(S("indices"), 1)

            def dots(j, turn=0):
                b = j % TB
                few = e["few"][:, j * 96:(j + 1) * 96]
                for k in range(TK):
                    g = j * TK + k
                    dve.wait_ge(S(f"u_landed{g % RU}"), turn * (TK * 16 // RU) + 16 * (g // RU + 1))
                    own(v.tensor_tensor_reduce(out=e["junk"], in0=ubuf[:, g % RU, :], in1=h2[:, b, :], scale=1.0,
                                               scalar=0.0, op0=ALU.mult, op1=ALU.add, accum_out=few[:, 32 + k:33 + k]))
                    dve.sem_inc(S("dotted"), 1)

            def weigh(j, turn=0):
                few = e["few"][:, j * 96:(j + 1) * 96]
                dve.wait_ge(S("gates_exp"), turn + (j + 1))
                own(v.reciprocal(few[:, 18:19], few[:, 16:17]))
                dve.wait_ge(S("gelu_ready"), turn + (j + 1))
                v.scalar_tensor_tensor(few[:, 64:80], few[:, 48:64], few[:, 18:19], few[:, 0:16], ALU.mult, ALU.mult
                                       ).then_inc(S("weights"), 1)

            dve.wait_ge(S("turned_copied"), 4)
            for j in range(AHEAD):
                choose(j, j // TB)

            def expert_turn(i, last):
                turn = i * UB
                for j in range(UB):
                    dots(j, turn)
                    weigh(j, turn)
                    if not last or j + AHEAD < UB:
                        choose(j + AHEAD, i * (UB // TB) + (j + AHEAD) // TB, turn)

            turns = UNITS // UB
            before = own.n
            expert_turn(0, False)
            per_turn = own.n - before
            with dve.Fori(1, turns - 1) as i:
                own.loop(i - 1, per_turn)
                expert_turn(i, False)
            own.end(turns - 2)
            expert_turn(turns - 1, True)

            dve.wait_ge(S("turned_copied"), 6)
            dve.wait_ge(S("residual_turned"), 1)
            dve.wait_ge(S("final_landed"), 16)
            for b in range(TB):
                dve.wait_ge(S("weighed"), UNITS * TK - (TB - 1 - b) * TK)
                own(v.tensor_tensor(e["junk"], ps[:, 4 + 2 * b:6 + 2 * b, :].rearrange("p a n -> p (a n)"), gtrow, ALU.mult))
                v.tensor_tensor(ubuf[:, b, :], e["junk"], ps[:, 2 * b:2 * b + 2, :].rearrange("p a n -> p (a n)"), ALU.add).then_inc(S("summed"), 1)
                dve.wait_ge(S("last_std"), b + 1)
                own(v.reciprocal(lb[:, 6 + b, 1:2], lb[:, 6 + b, 0:1]))
                v.scalar_tensor_tensor(ubuf[:, b, :], ubuf[:, b, :], lb[:, 6 + b, 1:2], fgrow, ALU.mult, ALU.mult
                                       ).then_inc(S("out_ready"), 1)

        @block.gpsimd
        def _(pool):
            g = nc.gpsimd
            own = Chain(pool, S("pool_own"), S("pool_waited"))
            g.memset(eps[:, :], EPS)
            g.memset(zeros[:, :], 0.0)
            g.memset(ones[:, :], 1.0).then_inc(S("constants"), 2)

            pool.wait_ge(S("slots_done"), S_IN)
            g.memset(m["sc"], 0.0).then_inc(S("scores_zeroed"), 1)

            pool.wait_ge(S("slots_done"), S_PLE)
            pool.wait_ge(S("ple_ready"), 4)
            for name in ("up", "s1", "s2", "s4", "s8"):
                g.memset(s[name], 0.0)
            g.memset(s["qp"], 0.0)
            own(g.memset(s["kp"], 0.0))
            pool.sem_inc(S("padded"), 1)

            pool.wait_ge(S("small_landed"), 16 * 5)
            pool.wait_ge(S("banks_freed"), S_IN2 + 14)
            t0 = 16
            for dst, src, first, lag in ((s1, up, 0, 1), (s2, s1, 1, 2), (s4, s2, 1, 4), (s8, s4, 1, 8)):
                n = dst.shape[1]
                own(g.tensor_tensor(dst[:, :, t0:t0 + T], src[:, first:first + n, t0:t0 + T],
                                    src[:, first:first + n, t0 - lag:t0 - lag + T], ALU.add))
            for k, src in enumerate((s1, s2, s4, s8)):
                own(g.tensor_tensor(pooled[:, k, :], src[:, 0, t0:t0 + T], inv_count[:, k, :], ALU.mult))
            g.tensor_tensor(pooled[:, :, :], pooled[:, :, :], up[:, :, t0:t0 + T], ALU.subtract).then_inc(S("pooled"), 1)

            def fetch(j, turn, table, to, ring_size, landed, used):
                q = j % UB
                few = e["few"][:, q * 96:(q + 1) * 96]
                pool.wait_ge(S("indices"), turn + (j + 1))
                for k in range(TK):
                    row = j * TK + k
                    if not (isinstance(turn, int) and turn * TK + row < ring_size):
                        pool.wait_ge(S(used), turn * TK + (row - ring_size + 1))
                        own.apart()
                    g.indirect_dma_start(to[:, row % ring_size, :], None, table,
                                         bass.IndirectOffsetOnAxis(ap=few[:, 80 + k:81 + k].bitcast(U32), axis=0)
                                         ).then_inc(S(f"{landed}{row % ring_size}"), 16)

            def fetch_u(j, turn=0):
                fetch(j, turn, a["expert_u"], ubuf, RU, "u_landed", "dotted")

            def fetch_v(j, turn=0):
                fetch(j, turn, a["expert_v"], vbuf, RV, "v_landed", "weighed")

            def expert_turn(turn, last):
                for j in range(UB):
                    if not last or j + 1 < UB:
                        fetch_u(j + 1, turn)
                    fetch_v(j, turn)

            fetch_u(0)
            expert_turn(0, False)
            with pool.Fori(1, UNITS // UB - 1) as i:
                expert_turn(i * UB, False)
            expert_turn(UNITS - UB, True)


TURN = (6.28125, 0.0019350051879882812, 3.01991598e-07)
TURN_INV = float(1.0 / (2.0 * np.pi))
HALF_TURN = 3.1415925
ROUND = float(1.5 * 2 ** 23)


def constants():
    con = np.zeros((P, N_CON), np.float32)

    def put(name, value, rows=P):
        con[:rows, CON[name][0]:CON[name][1]] = value

    put("ident", np.eye(P))
    swap = np.zeros((ROPE, ROPE))
    half = ROPE // 2
    for i in range(half):
        swap[i + half, i] = -1.0
        swap[i, i + half] = 1.0
    put("swap", swap, ROPE)
    tri = np.where(np.arange(P)[:, None] >= np.arange(P)[None, :], 0.0, NEG)
    put("causal", np.concatenate([np.zeros((P, P)), tri], 1))
    put("iota", np.arange(TK)[None, :])
    inv = (10000.0 ** (-np.arange(half, dtype=np.float64) / half)).astype(np.float32)
    put("inv_freq", np.concatenate([inv, inv])[:, None], ROPE)
    rows = np.arange(P) % 64
    put("is_value", (rows < AH)[:, None].astype(np.float32))
    put("not_value", ((rows >= AH) & (rows < 2 * AH))[:, None].astype(np.float32))
    put("sel_q", (rows[:, None] == AH + np.arange(AH)[None, :]).astype(np.float32))
    put("sel_k", (rows[:, None] == np.arange(AH)[None, :]).astype(np.float32))

    at = np.arange(P)
    masks = np.zeros((P, LEVELS + 1, P), np.int32)
    masks[:, 0] = np.eye(P)
    for n in range(LEVELS):
        sb, tb = at[:, None] >> n, at[None, :] >> n
        masks[:, n + 1] = (sb % 2 == 0) & (tb == sb + 1)
    inv_count = np.stack([1.0 / np.minimum(np.arange(T) + 1, 2 ** (g + 1)) for g in range(4)]).astype(np.float32)
    return con, masks, inv_count.reshape(1, 4 * T)


def kernel(**inputs):
    import concourse.bacc as bacc
    from concourse.bass_utils import run_bass_kernel_spmd

    x = {k: np.asarray(v) for k, v in inputs.items()}

    def slots(w, width=T):
        k, n = w.shape[0] // P, w.shape[1] // width
        return w.reshape(k, P, n, width).transpose(2, 1, 0, 3).reshape(n, P, k * width)

    def by_feature(w):
        return w.reshape(-1, P).T

    w_in, w_in2 = x["w_in"][0], x["w_in_2"][0]
    gate1, up1, mod = (slots(x[n][0]) for n in ("w1_gate", "w1_up", "w_mod_2"))
    gate2, up2 = slots(x["w2_gate"][0]), slots(x["w2_up"][0])
    w8 = []
    for b in range(FB):
        w8 += [gate1[b], up1[b]]
    latent = np.concatenate([w_in[:, 2048:2496], np.zeros((D, 64), np.float32)], 1)
    w8 += list(slots(np.concatenate([w_in[:, 512:1024], w_in[:, 0:512], latent, w_in[:, 1024:2048]], 1)))
    w8 += list(slots(x["w_out"][0]))
    for b in range(FB):
        w8 += [gate2[b], up2[b]]
    w8 += list(slots(x["w_ple_gate"][0]))
    w8 += list(slots(np.concatenate([w_in2[:, 512:3584], w_in2[:, 0:512], w_in2[:, 3600:5648]], 1)))
    w8 += list(slots(x["w_out_2"][0]))
    w8 += list(slots(x["peer_w_query_2"][0]))
    w22 = np.concatenate([slots(x["w1_down"][0], P), slots(x["w2_down"][0], P)])

    con, masks, inv_count = constants()
    f_cols = w_in2[:, 3584:3600]
    wf = np.zeros((D, 96), np.float32)
    b_f = np.zeros((P, 1), np.float32)
    for at in (0, 16, 64, 80):
        wf[:, at:at + AH] = f_cols
        b_f[at:at + AH, 0] = x["b_f_2"][0]
    table = {"ffn1": "ln_ffn1", "mix": "ln_mix", "ffn2": "ln_ffn2", "ple": "ln_ple", "final1": "ln_final",
             "norm1": "norm1_g_2", "norm2": "norm2_g_2", "pool_scale": "pool_scale_2", "hg_norm": "hg_out_norm",
             "q_a": "q_a_norm", "kv_a": "kv_a_norm", "lb": "hg_lb_logits", "c": "c_2", "b_mod": "b_mod_2"}
    vec = np.concatenate([b_f if n == "b_f" else by_feature(x[table[n]]) for n in VEC], 1)
    small = np.concatenate([slots(x["w_q_up"][0], HH * QK)[0], x["w_kv_up"][0], slots(x["w_ple_proj"][0], D)[0],
                            x["w_pool_2"][0].transpose(1, 0, 2).reshape(P, 4 * T)], 1)
    arrays = {
        "x": slots(x["x"][0].T)[0].reshape(P, C, T),
        "p": slots(x["p"][0, 0].T)[0].reshape(P, 2, T),
        "pos": x["positions"].reshape(1, T).astype(np.int32),
        "vec": vec, "con": con, "lev_mask": masks, "inv_count": inv_count,
        "w8": np.stack(w8), "wmod": mod, "w22": w22, "small": small,
        "wf": slots(wf, 96)[0].reshape(P, C, 96),
        "keys": x["peer_sub_keys_2"][0].reshape(2 * PH, NK, P).transpose(2, 0, 1),
        "expert_u": x["peer_u_2"][0], "expert_v": x["peer_v_2"][0],
        "final_g": x["final_g_2"].reshape(1, D),
    }
    nc = bacc.Bacc("TRN2", target_bir_lowering=False, num_devices=1)
    feeds, aps = {}, {}
    for name, value in arrays.items():
        value = np.ascontiguousarray(value)
        feeds[f"in_{name}"] = value
        aps[name] = nc.dram_tensor(f"in_{name}", value.shape, mybir.dt.from_np(value.dtype), kind="ExternalInput").ap()
    out = nc.dram_tensor("out", (T, D), F32, kind="ExternalOutput").ap()
    program(nc, aps, out)
    result = run_bass_kernel_spmd(nc, [feeds], core_ids=[0])
    return result.results[0]["out"].reshape(1, T, D)
```

```python
from contextlib import ExitStack

import numpy as np

import concourse.bass as bass
from concourse import mybir

P = 128
T = 256
TB = T // P
D = 1024
C = D // P
FF = 2816
FC = FF // P
FB = FF // T
HH = 4
ROPE = 64
QK = 128 + ROPE
AH = 16
AD = 64
PH = 8
NK = 128
TK = 16
EPS = 1e-6
SLOT = C * T
TILE = SLOT // 2
RAW = 2
TILES = 4
BANKS = 4
MODS = 6 * D // T
MOD_RING = 2
NEG = -3.0e38
LEVELS = 7
RU = 8
RV = 8
UB = 4
UNITS = PH * TB
ARENA = 18608
AHEAD_Q = 4
AHEAD = 2

F32 = mybir.dt.float32
F32R = mybir.dt.float32r
I32 = mybir.dt.int32
U32 = mybir.dt.uint32
ALU = mybir.AluOpType
ACT = mybir.ActivationFunctionType
AX = mybir.AxisListType.X

S_FFN1 = 0
S_DOWN1 = S_FFN1 + 2 * FB
S_IN = S_DOWN1 + C
N_IN = 10
S_OUT = S_IN + N_IN
S_FFN2 = S_OUT + 4
S_DOWN2 = S_FFN2 + 2 * FB
S_PLE = S_DOWN2 + C
S_IN2 = S_PLE + 4
N_IN2 = 22
S_OUT2 = S_IN2 + N_IN2
S_PQ = S_OUT2 + 4
S_END = S_PQ + PH

DOWN_SLOTS = C * FC // (2 * C)


def weight_slot(n):
    return n + (DOWN_SLOTS - C) * ((n >= S_IN) + (n >= S_PLE))


W_END = weight_slot(S_END)


def tiles_after(n):
    for first in (S_DOWN1, S_DOWN2):
        if first <= n < first + C:
            return 2 * weight_slot(first) + -(-FC * (n - first + 1) // C)
    return 2 * weight_slot(n) + 2


def on_vector(tile):
    n = tile // 2
    busy = any(weight_slot(lo) <= n < weight_slot(hi) for lo, hi in ((S_IN + 2, S_OUT + 2), (S_IN2 + 2, S_END)))
    busy = busy or n in (weight_slot(S_DOWN1) + 2, weight_slot(S_DOWN2) + 2)
    return tile % 2 == 0 and not busy


def low_part(tile):
    mine = on_vector(tile)
    return "low_dve" if mine else "low_pool", sum(on_vector(t) == mine for t in range(tile + 1))


def columns(widths):
    at, out = 0, {}
    for name, width in widths:
        out[name] = (at, at + width)
        at += width
    return out, at


VEC, N_VEC = columns([("ffn1", C), ("mix", C), ("ffn2", C), ("ple", C), ("final1", C), ("norm1", C),
                      ("norm2", C), ("pool_scale", C), ("hg_norm", HH), ("q_a", 2), ("kv_a", 1),
                      ("lb", 2 * HH), ("c", C), ("b_mod", 6 * C), ("b_f", 1)])
CON, N_CON = columns([("ident", P), ("swap", ROPE), ("causal", 2 * P), ("iota", TK), ("inv_freq", 1),
                      ("is_value", 1), ("not_value", 1), ("sel_q", AH), ("sel_k", AH)])
SMALL, N_SMALL = columns([("w_q_up", 2 * HH * QK), ("w_kv_up", HH * 2 * P), ("w_ple", 2 * D),
                          ("w_pool", 4 * T)])


class Chain:

    def __init__(self, eng, sem, apart):
        self.eng, self.sem, self.waited, self.n, self.turn = eng, sem, apart, 0, 0

    def __call__(self, ins, apart=False):
        self.n += 1
        ins.then_inc(self.sem, 1)
        self.eng.wait_ge(self.sem, self.turn + self.n)
        if apart:
            self.apart()

    def apart(self):
        self.eng.sem_inc(self.waited, 1)

    def loop(self, i, per):
        self.turn, self.start, self.per = i * per, self.n, per

    def end(self, turns):
        assert self.n - self.start == self.per, (self.n - self.start, self.per)
        self.n, self.turn = self.start + turns * self.per, 0


def program(nc, a, out):
    with ExitStack() as ctx:
        sems = {}

        def S(name):
            if name not in sems:
                sems[name] = ctx.enter_context(nc.semaphore(name))
            return sems[name]

        def sb(name, shape, dt=F32):
            return ctx.enter_context(nc.sbuf_tensor(name, shape, dt))

        ps = ctx.enter_context(nc.psum_tensor("ps", [P, 8, 512], F32))
        ring = sb("ring", [P, RAW, SLOT])
        vec = sb("vec", [P, N_VEC])
        con = sb("con", [P, N_CON])
        small = sb("small", [P, N_SMALL])
        keys = sb("keys", [P, 2 * PH, P])
        wf = sb("wf", [P, C, 96])
        lev_mask = sb("lev_mask", [P, LEVELS + 1, P], I32)
        inv_count = sb("inv_count", [P, 4, T])
        h = sb("h", [P, C, T])
        sq = sb("sq", [P, C, T])
        ones = sb("ones", [P, P])
        zeros = sb("zeros", [P, P])
        pT = sb("pT", [P, 2, T])
        eps = sb("eps", [P, 1])
        std = sb("std", [P, 2, T])
        rstd = sb("rstd", [P, 2, T])
        mod = sb("mod", [P, 6 * C])
        coef = sb("coef", [P, 2 * C])
        silu = sb("silu", [P, 2, T])
        lb = sb("lb", [P, 8, HH])
        cos = sb("cos", [ROPE, T])
        sin = sb("sin", [ROPE, T])
        with nc.sbuf_tensor("v_rows", [P, RV, D], F32) as vbuf:
            pass
        whi = sb("whi", [P, TILES, TILE], F32R)
        wlo = sb("wlo", [P, TILES, TILE], F32R)
        with nc.sbuf_tensor("diag", [P, TK, P], F32) as diag:
            pass
        nh = sb("nh", [P, C, T], F32R)
        nl = sb("nl", [P, C, T], F32R)
        with nc.sbuf_tensor("arena", [P, ARENA], F32) as arena:
            pass
        gh = sb("gh", [P, FC, T], F32R)
        gl = sb("gl", [P, FC, T], F32R)

        def carve(widths):
            at, views = 0, {}
            for name, width in widths:
                views[name] = arena[:, at:at + width]
                at += width
            assert at <= ARENA, at
            return views

        def heads(ap, n):
            return ap.rearrange("p (h t) -> p h t", h=n)

        def V(name, j=0, n=1):
            lo = VEC[name][0] + j
            return vec[:, lo:lo + n]

        def K(name, rows=P):
            lo, hi = CON[name]
            return con[0:rows, lo:hi]

        ident = K("ident")
        w_q_up = small[:, slice(*SMALL["w_q_up"])].rearrange("p (k n) -> p k n", k=2)
        w_kv_up = small[:, slice(*SMALL["w_kv_up"])].rearrange("p (h n) -> p h n", h=HH)
        w_ple = small[:, slice(*SMALL["w_ple"])].rearrange("p (k n) -> p k n", k=2)
        w_pool = small[:, slice(*SMALL["w_pool"])].rearrange("p (g n) -> p g n", g=4)

        ff = carve([("gu", 2 * FC * T), ("wm", MOD_RING * SLOT), ("sum", MOD_RING * T), ("ang", 4 * T), ("pos", T)])
        wm = ff["wm"].rearrange("p (r k n) -> p r k n", r=MOD_RING, k=C)
        mod_sum = heads(ff["sum"], MOD_RING)
        ang, posi = heads(ff["ang"], 4)[0:ROPE], ff["pos"][0:ROPE].bitcast(I32)

        m = carve([("q", 1024), ("k", 1024), ("qf", 1024), ("sc", 1024), ("b0", 1024), ("b1", 1024), ("v", 1024),
                   ("g", 1024), ("cq", 768), ("cqn", 768), ("xr", 1280), ("rot", 1280), ("qn", 1024), ("kn", 1024),
                   ("va", 1024), ("prT", 1536), ("st", 64)])
        m["o"] = m["q"]
        m["sc7"] = m["cq"][:, 0:512]
        m["pr"] = arena[:, 4096:4096 + 1536]
        hq, hk, hqf = heads(m["q"], HH), heads(m["k"], HH), heads(m["qf"], HH)
        scT = m["sc"].rearrange("p (h b t) -> p h b t", h=HH, b=TB)
        sc7 = heads(m["sc7"], HH)
        hv = m["v"].rearrange("p (b n) -> p b n", b=TB)
        hg, ho = heads(m["g"], HH), heads(m["o"], HH)
        csq, osq, ostd = sq[:, 0:3, :], sq[:, 0:HH, :], sq[:, HH:C, :]
        cq, cqn = heads(m["cq"], 3), heads(m["cqn"], 3)
        xr, rot, rt = (heads(x, HH + 1) for x in (m["xr"], m["rot"], m["prT"][:, 0:(HH + 1) * T]))
        qn, kn = heads(m["qn"], HH), heads(m["kn"], HH)
        va = m["va"].rearrange("p (b n) -> p b n", b=TB)
        mixed = sq

        s = carve([("qp", AH * T), ("kp", AH * T), ("v", TB * D), ("ga", C * T), ("gb", C * T),
                   ("pr", 1536), ("prT", 1536), ("st", 64)])
        s["f"] = s["prT"]
        qp, kp = heads(s["qp"], AH), heads(s["kp"], AH)
        v2 = s["v"].rearrange("p (b n) -> p b n", b=TB)
        ga, gb, o2 = heads(s["ga"], C), heads(s["gb"], C), sq
        at = 0
        for name, groups in (("up", 4), ("s1", 4), ("s2", 3), ("s4", 2), ("s8", 1)):
            s[name] = small[:, at:at + groups * 272]
            at += groups * 272
        up, s1, s2, s4, s8 = (s[x].rearrange("p (g t) -> p g t", t=272) for x in ("up", "s1", "s2", "s4", "s8"))
        pooled = s1[:, :, 16:16 + T]
        fl = heads(s["f"], 6)

        e = carve([("qT", 4 * T), ("U", RU * D), ("h2", TB * D), ("junk", D), ("wk", 3 * 256), ("oh", 2 * 256),
                   ("vals", UB * 64), ("sel", 32), ("few", UB * 96)])
        qT = heads(e["qT"], 4)
        h2 = e["h2"].rearrange("p (b n) -> p b n", b=TB)
        gtrow, fgrow = small[:, PH * 512:PH * 512 + D], lev_mask[:, :, :].rearrange("p l t -> p (l t)").bitcast(F32)
        gtb = inv_count[:, :, :].rearrange("p g t -> p (g t)").rearrange("p (c t) -> p c t", c=C)
        ubuf = heads(e["U"], RU)
        scores = small[:, 0:PH * 512].rearrange("p (h b n) -> p h b n", h=PH, b=TB)

        def pair(r):
            return ps[:, r, :].rearrange("p (t n) -> p t n", t=2)

        def blocks(ap):
            return ap.rearrange("p (k n) -> p k n", k=C)

        block = ctx.enter_context(nc.Block())

        def low(v, eng, tile, turn=0):
            eng.wait_ge(S("high_w"), turn * 2 + tile + 1)
            at = (tile % 2) * TILE
            return v.tensor_tensor(wlo[:, tile % TILES, :], ring[:, tile // 2 % RAW, at:at + TILE],
                                   whi[:, tile % TILES, :].bitcast(F32), ALU.subtract)

        @block.sync
        def _(sp):
            def row(src, at):
                return src[at, :, :] if isinstance(at, int) else src[bass.ds(at, 1), :, :].rearrange("a p n -> p (a n)")

            def load(slot, turn=0):
                r, src = slot % RAW, row(a["w"], turn + slot)
                if slot >= RAW:
                    for t in range(2):
                        name, n = low_part(2 * (slot - RAW) + t)
                        sp.wait_ge(S(name), turn + n)
                        if not isinstance(turn, int):
                            sp.sem_inc(S("sp_waited"), 1)
                sp.dma_start(ring[:, r, :], src).then_inc(S(f"landed{r}"), 16)

            def load_mod(j, turn=0):
                r, src = j % MOD_RING, row(a["wmod"], turn + j)
                if j >= MOD_RING or not isinstance(turn, int):
                    sp.wait_ge(S("mod_summed"), turn + (j - MOD_RING + 1))
                sp.dma_start(wm[:, r, :, :].rearrange("p k n -> p (k n)"), src
                             ).then_inc(S(f"mod_landed{r}"), 16)

            def swiglu(slot, mod):
                load_mod(mod)
                turns = FB // 2

                def turn(i):
                    for j in range(4):
                        load(slot + RAW + j, i * 4)
                        if j % 2:
                            load_mod(mod + 1 + j // 2, i * 2)

                turn(0)
                with sp.Fori(1, turns) as i:
                    turn(i)
                ahead = slot + RAW + turns * 4
                load(ahead)
                load_mod(mod + 1 + 2 * turns)
                for j in range(ahead + 1, slot + 2 * FB + DOWN_SLOTS + RAW):
                    load(j)

            load(0)
            load(1)
            swiglu(0, 0)
            for slot in range(weight_slot(S_IN) + RAW, weight_slot(S_FFN2) + RAW):
                load(slot)
            sp.wait_ge(S("tiles_done"), tiles_after(S_OUT))
            swiglu(weight_slot(S_FFN2), MODS // 2)
            for slot in range(weight_slot(S_PLE) + RAW, W_END):
                load(slot)
            for b in range(TB):
                sp.wait_ge(S("out_ready"), b + 1)
                sp.dma_start(out[b * P:(b + 1) * P, :], ubuf[:, b, :]).then_inc(S("stored"), 16)
            sp.wait_ge(S("stored"), 16 * TB)

        @block.tensor
        def _(pe):
            mm = nc.tensor.matmul

            def bank(n, turn=0):
                if n >= BANKS:
                    pe.wait_ge(S("banks_freed"), turn + (n - BANKS + 1))
                return n % BANKS

            def split_tile(tile, turn=0):
                name, n = low_part(tile)
                pe.wait_ge(S(name), turn + n)
                return blocks(whi[:, tile % TILES, :]), blocks(wlo[:, tile % TILES, :])

            def features(n, turn=0, split_at=None):
                r = bank(n, turn)
                for t in range(2):
                    tile = 2 * weight_slot(n) + t
                    hi, lo = split_tile(tile, turn)
                    to = pair(r)[:, t, :]
                    for k in range(C):
                        if split_at is not None and t == 0:
                            pe.wait_ge(S("high_x"), split_at * C + k + 1)
                        mm(to, hi[:, k, :], nh[:, k, :], start=(k == 0), stop=False)
                        mm(to, lo[:, k, :], nh[:, k, :], start=False, stop=False)
                    for k in range(C):
                        if split_at is not None and t == 0:
                            pe.wait_ge(S("low_x"), split_at * C + k + 1)
                        last = mm(to, hi[:, k, :], nl[:, k, :], start=False, stop=(k == C - 1))
                    last.then_inc(S("tiles_done"), 1)

            def tokens(n):
                r = bank(n)
                tile = 2 * weight_slot(n)
                split_tile(tile)
                split_tile(tile + 1)
                at = tile % TILES
                hi, lo = (w[:, at:at + 2, :].rearrange("p t (k n) -> p t k n", k=C) for w in (whi, wlo))
                for b in range(TB):
                    for k in range(C):
                        cols = slice(b * P, (b + 1) * P)
                        to = pair(r)[:, b, :]
                        mm(to, nh[:, k, cols], hi[:, :, k, :], start=(k == 0), stop=False)
                        mm(to, nh[:, k, cols], lo[:, :, k, :], start=False, stop=False)
                        last = mm(to, nl[:, k, cols], hi[:, :, k, :], start=False, stop=(k == C - 1))
                last.then_inc(S("tiles_done"), 2)

            def modulation(n, turn=0):
                pe.wait_ge(S("mod_summed"), turn + (n + MOD_RING))
                for j in range(2 * MOD_RING):
                    to = ps[:, 7, 2 * n + j:2 * n + j + 1] if isinstance(turn, int) else \
                        ps[:, 7, bass.ds(turn * 2 + (2 * n + j), 1)]
                    last = mm(to, mod_sum[:, j // 2, (j % 2) * P:(j % 2 + 1) * P], ones[:, 0:1], start=True, stop=True)
                last.then_inc(S("mod_read"), 1)

            def square_sum(m, c):
                pe.wait_ge(S("squared"), m * C + c + 1)
                if c == 0 and m:
                    pe.wait_ge(S("std_ready"), m)
                last = mm(ps[:, 4, 0:T], ones[:, :], sq[:, c, :], start=(c == 0), stop=(c == C - 1))
                if c == C - 1:
                    last.then_inc(S("sum_ready"), 1)

            def swiglu(n, mod, blocks_before, m, split_at):
                turns = FB // 2
                features(n, split_at=split_at)
                for j in range(1, 4):
                    features(n + j)
                with pe.Fori(1, turns) as i:
                    for j in range(4):
                        features(n + j, i * 4)
                        if j == 1:
                            modulation(mod - MOD_RING, i * 2)
                for j in range(turns * 4, 2 * FB):
                    features(n + j)
                first = n + 2 * FB
                for j in range(C):
                    r = bank(first + j)
                    to = ps[:, r, 0:T]
                    for k in range(FC):
                        if j == 0 and (k == 0 or k == FC - 2):
                            pe.wait_ge(S("low_gu"), blocks_before + FB - (k == 0))
                        at = j * FC + k
                        tile = 2 * weight_slot(first) + at // C
                        if at % C == 0:
                            hi, lo = split_tile(tile)
                        w = at % C
                        mm(to, hi[:, w, :], gh[:, k, :], start=(k == 0), stop=False)
                        mm(to, lo[:, w, :], gh[:, k, :], start=False, stop=False)
                        last = mm(to, hi[:, w, :], gl[:, k, :], start=False, stop=(k == FC - 1))
                        if w == C - 1:
                            last.then_inc(S("tiles_done"), 1)
                    if j in (0, 2):
                        modulation(mod + (turns - 1) * MOD_RING + j)
                    if j >= 2:
                        square_sum(m, j - 2)
                square_sum(m, C - 2)
                square_sum(m, C - 1)

            def residual(slot, split_at, m, extra=None):
                for j in range(4):
                    features(slot + j, split_at=None if j else split_at)
                    if extra:
                        extra(j)
                    if j >= 1:
                        square_sum(m, 2 * j - 2)
                        square_sum(m, 2 * j - 1)
                square_sum(m, C - 2)
                square_sum(m, C - 1)

            def attention(n, score, value, out_banks):
                if n >= 1:
                    pe.wait_ge(S("probsT_copied"), n)
                for hd in range(4):
                    score(hd, 0, ps[:, 5, hd * P:(hd + 1) * P])
                for hd in range(4):
                    last = score(hd, 1, ps[:, 6 + hd // 2, (hd % 2) * T:(hd % 2 + 1) * T])
                last.then_inc(S("scores_ready"), 1)
                return lambda: values(n, value, out_banks)

            def values(n, value, probs):
                pe.wait_ge(S("probs_ready"), n + 1)
                for hd in range(4):
                    nc.tensor.transpose(ps[:, 5, hd * P:(hd + 1) * P], probs[:, hd * P:(hd + 1) * P], ident)
                for b in range(TB):
                    for hd in range(4):
                        at = 512 + hd * T + b * P
                        last = nc.tensor.transpose(ps[:, 6 + b, hd * P:(hd + 1) * P], probs[:, at:at + P], ident)
                last.then_inc(S("probsT_ready"), 1)
                pe.wait_ge(S("probsT_copied"), n + 1)
                if n >= 1:
                    pe.wait_ge(S("attended_read"), n)
                for hd in range(4):
                    last = value(hd)
                last.then_inc(S("attended"), 1)

            pe.wait_ge(S("constants"), 2)
            pe.wait_ge(S("vec_landed"), 32)
            for c in range(C):
                square_sum(0, c)

            swiglu(S_FFN1, 0, 0, 1, 0)

            def level(n, q, k):
                pe.wait_ge(S("level_operands"), n + 1)
                if n == 0:
                    pe.wait_ge(S("std_ready"), 2)
                else:
                    pe.wait_ge(S("level_read"), n)
                for hd in range(HH):
                    for b in range(TB):
                        at = slice(b * P, (b + 1) * P)
                        last = mm(ps[:, 4 + hd // 2, (hd % 2 * 2 + b) * P:(hd % 2 * 2 + b + 1) * P],
                                  k[:, hd, at], q[:, hd, at], start=True, stop=True)
                last.then_inc(S("level_ready"), 1)

            def latent(n):
                if 2 <= n <= 10:
                    pe.wait_ge(S("latent_copied"), n - 1)
                return ps[:, 6 + n % 2, :].rearrange("p (t n) -> p t n", t=2)

            def latent_sums():
                pe.wait_ge(S("latent_squared"), 2)
                to = latent(0)
                mm(to[:, 0, :], ones[:, :], csq[:, 0, :], start=True, stop=False)
                mm(to[:, 0, :], ones[:, :], csq[:, 1, :], start=False, stop=True)
                mm(to[:, 1, :], ones[:, :], csq[:, 2, :], start=True, stop=True).then_inc(S("latent_ready"), 1)

            def q_up(n):
                to = latent(n)
                width, off = (P, 0) if n < 3 else (ROPE, P)
                if n == 1:
                    pe.wait_ge(S("latent_normed"), 1)
                for j in range(2):
                    hd = (n - 1) % 2 * 2 + j
                    for k in range(2):
                        last = mm(to[0:width, j, :], w_q_up[:, k, hd * QK + off:hd * QK + off + width],
                                  cqn[:, k, :], start=(k == 0), stop=(k == 1))
                last.then_inc(S("latent_ready"), 1)

            def k_up(n):
                to = latent(n)
                if n == 5:
                    pe.wait_ge(S("latent_normed"), 2)
                for j in range(2):
                    last = mm(to[:, j, :], w_kv_up[:, (n - 5) * 2 + j, 0:P], cqn[:, 2, :], start=True, stop=True)
                last.then_inc(S("latent_ready"), 1)

            def v_up(n):
                to = latent(n)
                b = n - 7
                mm(to.rearrange("p t n -> p (t n)"), cqn[:, 2, b * P:(b + 1) * P], w_kv_up[:, :, P:2 * P],
                   start=True, stop=True).then_inc(S("latent_ready"), 1)

            def swapped(n):
                to = latent(n)
                j = (n - 9) * 2
                if n == 9:
                    pe.wait_ge(S("latent_copied"), 9)
                if n == 11:
                    pe.wait_ge(S("rotated"), 1)
                width = min(2, HH + 1 - j) * T
                mm(to.rearrange("p t n -> p (t n)")[0:ROPE, 0:width], K("swap", ROPE),
                   xr[0:ROPE, j:j + width // T, :], start=True, stop=True).then_inc(S("latent_ready"), 1)

            features(S_IN, split_at=1)
            features(S_IN + 1)
            features(S_IN + 2)
            features(S_IN + 3)
            features(S_IN + 4)
            level(0, hq, hk)
            features(S_IN + 5)
            level(1, hqf, hk)
            tokens(S_IN + 6)
            latent_sums()
            level(2, hqf, hk)
            tokens(S_IN + 7)
            for n in (1, 2, 3, 4):
                q_up(n)
            level(3, hqf, hk)
            features(S_IN + 8)
            k_up(5)
            k_up(6)
            level(4, hqf, hk)
            features(S_IN + 9)
            v_up(7)
            v_up(8)
            level(5, hqf, hk)
            swapped(9)
            swapped(10)
            level(6, hqf, hk)
            swapped(11)
            level(7, hqf, hk)
            pe.wait_ge(S("level_operands"), LEVELS + 2)
            pe.wait_ge(S("level_read"), LEVELS + 1)
            for hd in range(HH):
                last = mm(ps[:, 4, hd * P:(hd + 1) * P], hk[:, hd, 0:P], hqf[:, hd, P:T], start=True, stop=True)
            last.then_inc(S("level_ready"), 1)
            pe.wait_ge(S("scores_built"), 1)
            pe.wait_ge(S("banks_freed"), S_OUT)
            for hd in range(HH):
                to = ps[:, hd // 2, (hd % 2) * T:(hd % 2 + 1) * T]
                cols = slice(hd * P, (hd + 1) * P)
                mm(to[:, 0:P], hv[:, 0, cols], scT[:, hd, 0, :], start=True, stop=True)
                mm(to[:, P:T], hv[:, 1, cols], scT[:, hd, 1, :], start=True, stop=False)
                last = mm(to[:, P:T], hv[:, 0, cols], sc7[:, hd, :], start=False, stop=True)
            last.then_inc(S("hg_out"), 1)

            def hg_sums():
                pe.wait_ge(S("hg_squared"), 1)
                for j in range(2):
                    last = mm(ps[:, 2 + j, :], ones[:, :], osq[:, 2 * j:2 * j + 2, :], start=True, stop=True)
                last.then_inc(S("hg_sums"), 1)

            def mla_score(hd, b, to):
                at, upto = slice(b * P, (b + 1) * P), (b + 1) * P
                mm(to, qn[:, hd, at], kn[:, hd, 0:upto], start=True, stop=False)
                return mm(to, rot[0:ROPE, hd, at], rot[0:ROPE, HH, 0:upto], start=False, stop=True)

            def mla_value(hd):
                to = ps[:, 5 + hd // 2, (hd % 2) * T:(hd % 2 + 1) * T]
                pt = m["prT"]
                cols = slice(hd * P, (hd + 1) * P)
                mm(to[:, 0:P], va[:, 0, cols], pt[:, cols], start=True, stop=True)
                mm(to[:, P:T], va[:, 0, cols], pt[:, 512 + hd * P:512 + (hd + 1) * P], start=True, stop=False)
                return mm(to[:, P:T], va[:, 1, cols], pt[:, 1024 + hd * P:1024 + (hd + 1) * P], start=False, stop=True)

            pe.wait_ge(S("rope_done"), 1)
            rest = attention(0, mla_score, mla_value, m["pr"])
            hg_sums()
            rest()

            pe.wait_ge(S("attended_read"), 1)
            pe.wait_ge(S("hg_gated"), 1)
            residual(S_OUT, 2, 2)
            swiglu(S_FFN2, MODS // 2, FB, 3, 3)

            def ple_product(j):
                if j == 0:
                    pe.wait_ge(S("p_landed"), 16)
                if j >= 2:
                    pe.wait_ge(S("ple_added"), j - 1)
                for t in range(2):
                    for k in range(2):
                        last = mm(ps[:, 5 + j % 2, t * T:(t + 1) * T], w_ple[:, k, (2 * j + t) * P:(2 * j + t + 1) * P],
                                  pT[:, k, :], start=(k == 0), stop=(k == 1))
                last.then_inc(S("ple_ready"), 1)

            residual(S_PLE, 4, 4, ple_product)
            for c in range(C):
                square_sum(5, c)

            pe.wait_ge(S("shifted"), C)
            pe.wait_ge(S("std_ready"), 6)
            for k in range(C):
                last = mm(ps[0:96, 5, 0:T], wf[:, k, :], sq[:, k, :], start=(k == 0), stop=(k == C - 1))
            last.then_inc(S("forget_ready"), 1)
            for base, step in ((S_IN2, features), (S_IN2 + 4, features), (S_IN2 + 8, tokens)):
                for j in range(4):
                    if base == S_IN2 and j == 0:
                        step(base, split_at=5)
                    else:
                        step(base + j)

            def fa_score(group):
                def score(hd, b, to):
                    head = 4 * group + hd
                    return mm(to, qp[:, head, b * P:(b + 1) * P], kp[:, head, 0:(b + 1) * P], start=True, stop=True)
                return score

            def fa_value(group):
                def value(hd):
                    head = 4 * group + hd
                    rows = slice((hd % 2) * AD, (hd % 2 + 1) * AD)
                    to = ps[rows, 4, (hd // 2) * T:(hd // 2 + 1) * T]
                    pt, cols = s["prT"], slice(head * AD, (head + 1) * AD)
                    mm(to[:, 0:P], v2[:, 0, cols], pt[:, hd * P:(hd + 1) * P], start=True, stop=True)
                    mm(to[:, P:T], v2[:, 0, cols], pt[:, 512 + hd * P:512 + (hd + 1) * P], start=True, stop=False)
                    return mm(to[:, P:T], v2[:, 1, cols], pt[:, 1024 + hd * P:1024 + (hd + 1) * P],
                              start=False, stop=True)
                return value

            pe.wait_ge(S("decay_rows"), 4)
            pe.wait_ge(S("banks_freed"), S_IN2 + 12)
            slot = S_IN2 + 12
            rest = attention(1, fa_score(0), fa_value(0), s["pr"])
            for group in range(4):
                for j in range(2):
                    features(slot)
                    slot += 1
                rest()
                if group < 3:
                    rest = attention(group + 2, fa_score(group + 1), fa_value(group + 1), s["pr"])
            features(slot)
            features(slot + 1)
            pe.wait_ge(S("pooled"), 1)
            pe.wait_ge(S("probsT_copied"), 5)
            for g in range(4):
                if g >= 2:
                    pe.wait_ge(S("pool_read"), g - 1)
                for t in range(2):
                    last = mm(ps[:, 5 + g % 2, t * T:(t + 1) * T], w_pool[:, g, t * P:(t + 1) * P], pooled[:, g, :],
                              start=True, stop=True)
                last.then_inc(S("pool_ready"), 1)
            pe.wait_ge(S("branches"), 1)
            residual(S_OUT2, 6, 6)

            def key_scores(hd):
                r = (S_PQ + hd) % BANKS
                pe.wait_ge(S("queries_copied"), hd + 1)
                for b in range(TB):
                    for p in range(2):
                        last = mm(ps[:, r, (2 * b + p) * P:(2 * b + p + 1) * P], qT[:, hd % 2 * 2 + p, b * P:(b + 1) * P],
                                  keys[:, 2 * hd + p, :], start=True, stop=True)
                last.then_inc(S("key_scores"), 1)

            turned = 0
            def turn_around(src, n):
                nonlocal turned
                if turned >= 2:
                    pe.wait_ge(S("turned_copied"), turned - 1)
                b, half = n // 2, n % 2
                for c in range(4):
                    last = nc.tensor.transpose(ps[:, 5 + turned % 2, c * P:(c + 1) * P],
                                               src[:, half * 4 + c, b * P:(b + 1) * P], ident)
                last.then_inc(S("turned"), 1)
                turned += 1

            features(S_PQ, split_at=7)
            for n in range(4):
                turn_around(sq, n)
            key_scores(0)
            for hd in range(1, PH):
                features(S_PQ + hd)
                if hd == 3:
                    pe.wait_ge(S("gate_columns"), 1)
                    for n in range(2):
                        if turned >= 2:
                            pe.wait_ge(S("turned_copied"), turned - 1)
                        for c in range(4):
                            last = nc.tensor.transpose(ps[:, 5 + turned % 2, c * P:(c + 1) * P],
                                                       gtb[:, n * 4 + c, :], ident)
                        last.then_inc(S("turned"), 1)
                        turned += 1
                key_scores(hd)
            pe.wait_ge(S("turned_copied"), 6)
            for b in range(4):
                mm(ps[:, 4 + b, :], zeros[:, :], keys[:, 0:4, :], start=True, stop=False, skip_group_check=True)

            def weigh(j, k, turn):
                acc = 4 + 2 * (j % TB)
                g = j * TK + k
                pe.wait_ge(S("diagonals"), turn * TK + (g + 1))
                pe.wait_ge(S(f"v_landed{g % RV}"), turn * (TK * 16 // RV) + 16 * (g // RV + 1))
                mm(ps[:, acc, :], diag[:, k, :], vbuf[:, g % RV, 0:512], start=False, stop=False,
                   skip_group_check=True)
                mm(ps[:, acc + 1, :], diag[:, k, :], vbuf[:, g % RV, 512:D], start=False, stop=False,
                   skip_group_check=True).then_inc(S("weighed"), 1)

            pe.wait_ge(S("banks_freed"), S_END)
            for b in range(TB):
                for c in range(C):
                    last = nc.tensor.transpose(ps[:, 2 * b + c // 4, (c % 4) * P:(c % 4 + 1) * P],
                                               h[:, c, b * P:(b + 1) * P], ident)
            last.then_inc(S("residual_turned"), 1)

            with pe.Fori(0, UNITS // UB) as i:
                for j in range(UB):
                    for k in range(TK):
                        weigh(j, k, i * UB)

        @block.scalar
        def _(act):
            fn = nc.scalar.activation
            own = Chain(act, S("act_own"), S("act_waited"))

            act.dma_start(h[:, :, :], a["x"]).then_inc(S("x_landed"), 16)
            act.dma_start(vec[:, :], a["vec"]).then_inc(S("vec_landed"), 16)
            act.dma_start(con[:, :], a["con"]).then_inc(S("vec_landed"), 16)
            act.dma_start(posi[:, :], a["pos"].partition_broadcast(ROPE).rearrange("p a t -> p (a t)")
                          ).then_inc(S("pos_landed"), 16)
            act.dma_start(wf[:, :, :], a["wf"]).then_inc(S("small_landed"), 16)
            act.dma_start(small[:, :], a["small"]).then_inc(S("small_landed"), 16)
            act.dma_start(lev_mask[:, :, :], a["lev_mask"]).then_inc(S("small_landed"), 16)
            act.dma_start(inv_count[:, :, :].rearrange("p g t -> p (g t)"),
                          a["inv_count"].partition_broadcast(P).rearrange("p a t -> p (a t)")
                          ).then_inc(S("small_landed"), 16)
            act.dma_start(keys[:, :, :], a["keys"]).then_inc(S("small_landed"), 16)
            act.dma_start(pT[:, :, :], a["p"]).then_inc(S("p_landed"), 16)

            def square(m, c):
                if m == 0:
                    act.wait_ge(S("x_landed"), 16)
                elif m == 5:
                    act.wait_ge(S("block1_out"), c + 1)
                else:
                    n = {1: S_DOWN1, 2: S_OUT, 3: S_DOWN2, 4: S_PLE, 6: S_OUT2}[m] + (c if m in (1, 3) else c // 2)
                    product(n)
                    act.wait_ge(S("banks_freed"), n + 1)
                if m:
                    act.wait_ge(S("sum_ready"), m)
                fn(sq[:, c, :], h[:, c, :], ACT.Square).then_inc(S("squared"), 1)

            def root(m):
                act.wait_ge(S("sum_ready"), m + 1)
                fn(std[:, 0, :], ps[:, 4, 0:T], ACT.Sqrt, bias=eps[:, 0:1], scale=1.0 / D).then_inc(S("std_ready"), 1)

            def shift(m, first):
                for c in range(C):
                    act.wait_ge(S("scaled"), (m - 5) * C + c + 1)
                    fn(sq[:, c, :], sq[:, c, :], ACT.Identity, bias=mod[:, first + c:first + c + 1]
                       ).then_inc(S("shifted"), 1)
                    if c:
                        act.wait_ge(S("shifted"), (m - 5) * C + c)
                        high_x(c - 1)
                act.wait_ge(S("shifted"), (m - 4) * C)
                high_x(C - 1)

            def high(tile, turn=0):
                slot = tile // 2
                if tile % 2 == 0:
                    act.wait_ge(S(f"landed{slot % RAW}"), turn * (16 // RAW) + 16 * (slot // RAW + 1))
                if tile >= TILES:
                    act.wait_ge(S("tiles_done"), turn * 2 + (tile - TILES + 1))
                at = (tile % 2) * TILE
                fn(whi[:, tile % TILES, :], ring[:, slot % RAW, at:at + TILE], ACT.Copy).then_inc(S("high_w"), 1)

            tile = 0

            def product(n, turn=0):
                nonlocal tile
                while tile < min(tiles_after(n) + TILES, 2 * W_END):
                    high(tile, turn)
                    tile += 1
                act.wait_ge(S("tiles_done"), turn * 2 + tiles_after(n))

            def high_x(c, x=sq):
                fn(nh[:, c, :], x[:, c, :], ACT.Copy).then_inc(S("high_x"), 1)

            def high_norm(m):
                for c in range(C):
                    act.wait_ge(S("normed"), m * C + c + 1)
                    high_x(c)

            act.wait_ge(S("constants"), 2)
            for c in range(C):
                square(0, c)
            while tile < 2:
                high(tile)
                tile += 1
            act.wait_ge(S("lb_shifted"), 1)
            fn(lb[:, 2:4, :], lb[:, 0:2, :], ACT.Exp).then_inc(S("lb_exp"), 1)
            act.wait_ge(S("angle"), 1)
            own(fn(sin[:, :], ang[:, 0, :], ACT.Sin))
            fn(cos[:, :], ang[:, 0, :], ACT.Sin, scale=0.5).then_inc(S("sines"), 1)
            root(0)

            high_norm(0)

            def gate(n, b, before, turn=0):
                product(n, turn)
                if not (isinstance(b, int) and b + before == 0):
                    act.wait_ge(S("low_gu"), b + before)
                fn(silu[:, :, :], pair(n % BANKS), ACT.Silu).then_inc(S("silu_ready"), 1)
                product(n + 1, turn)
                act.wait_ge(S("banks_freed"), turn + n + 2)
                fn(gh[:, 2 * b:2 * b + 2, :] if isinstance(b, int) else gh[:, bass.ds(b * 2, 2), :],
                   silu[:, :, :], ACT.Copy).then_inc(S("high_gu"), 1)

            def swiglu(n, before):
                nonlocal tile
                turns = FB // 2
                gate(n, 0, before)
                gate(n + 2, 1, before)
                tile -= 8
                with act.Fori(1, turns) as i:
                    gate(n, i * 2, before, i * 4)
                    gate(n + 2, i * 2 + 1, before, i * 4)
                tile += 8 * (turns - 1)
                gate(n + 4 * turns, 2 * turns, before)

            swiglu(S_FFN1, 0)
            for c in range(C):
                square(1, c)
            root(1)
            high_norm(1)

            def copied(slot, *ins):
                ins[-1].then_inc(S("banks_freed"), 1)

            act.wait_ge(S("banks_freed"), S_IN)
            for j in range(2):
                product(S_IN + j)
                fn(heads(m["b1"], HH)[:, 2 * j:2 * j + 2, :], pair((S_IN + j) % BANKS), ACT.Sigmoid)
                copied(S_IN + j, fn(hk[:, 2 * j:2 * j + 2, :], pair((S_IN + j) % BANKS), ACT.Sigmoid, scale=-1.0))
            for j in range(2):
                product(S_IN + 2 + j)
                copied(S_IN + 2 + j, fn(hq[:, 2 * j:2 * j + 2, :], pair((S_IN + 2 + j) % BANKS), ACT.Copy))
            product(S_IN + 4)
            copied(S_IN + 4, fn(cq[:, 0:2, :], pair((S_IN + 4) % BANKS), ACT.Copy))
            act.wait_ge(S("banks_freed"), S_IN + 5)
            fn(csq[:, 0:2, :], cq[:, 0:2, :], ACT.Square).then_inc(S("latent_squared"), 1)
            product(S_IN + 5)
            own(fn(cq[:, 2, :], pair((S_IN + 5) % BANKS)[:, 0, :], ACT.Copy))
            copied(S_IN + 5, fn(xr[0:ROPE, HH, :], pair((S_IN + 5) % BANKS)[0:ROPE, 1, :], ACT.Copy))
            fn(csq[:, 2, :], cq[:, 2, :], ACT.Square).then_inc(S("latent_squared"), 1)

            def values_out(j):
                product(S_IN + 6 + j)
                copied(S_IN + 6 + j, fn(hv[:, :, j * T:(j + 1) * T], pair((S_IN + 6 + j) % BANKS), ACT.Copy))

            def latent_out(n, to, rows=P):
                act.wait_ge(S("latent_ready"), n + 1)
                src = ps[0:rows, 6 + n % 2, :]
                fn(to, src if len(to.shape) == 2 else src.rearrange("p (t n) -> p t n", t=2), ACT.Copy
                   ).then_inc(S("latent_copied"), 1)

            values_out(0)
            act.wait_ge(S("latent_ready"), 1)
            own(fn(std[:, 0, :], ps[:, 6, 0:T], ACT.Sqrt, bias=eps[:, 0:1], scale=1.0 / (2 * P)))
            fn(std[:, 1, :], ps[:, 6, T:2 * T], ACT.Sqrt, bias=eps[:, 0:1], scale=1.0 / P).then_inc(S("latent_copied"), 1)
            values_out(1)
            latent_out(1, qn[:, 0:2, :])
            latent_out(2, qn[:, 2:4, :])
            latent_out(3, xr[0:ROPE, 0:2, :], ROPE)
            latent_out(4, xr[0:ROPE, 2:4, :], ROPE)

            def out_gate(j):
                product(S_IN + 8 + j)
                copied(S_IN + 8 + j, fn(hg[:, 2 * j:2 * j + 2, :], pair((S_IN + 8 + j) % BANKS), ACT.Silu))

            out_gate(0)
            latent_out(5, kn[:, 0:2, :])
            latent_out(6, kn[:, 2:4, :])
            out_gate(1)
            latent_out(7, va[:, 0, :])
            latent_out(8, va[:, 1, :])
            act.wait_ge(S("hg_out"), 1)
            fn(osq[:, :, :].rearrange("p h t -> p (h t)"), ps[:, 0:2, :].rearrange("p b n -> p (b n)"), ACT.Square
               ).then_inc(S("hg_squared"), 1)
            fn(m["o"], ps[:, 0:2, :].rearrange("p b n -> p (b n)"), ACT.Copy).then_inc(S("hg_copied"), 1)
            act.wait_ge(S("hg_sums"), 1)
            fn(ostd[:, :, :].rearrange("p h t -> p (h t)"), ps[:, 2:4, :].rearrange("p b n -> p (b n)"), ACT.Sqrt,
               bias=eps[:, 0:1], scale=1.0 / P).then_inc(S("hg_std"), 1)

            def exponentials(n, pr):
                act.wait_ge(S("logits"), n + 1)
                fn(pr, pr, ACT.Exp).then_inc(S("probs_exp"), 1)

            def turned_probs(n, prT):
                act.wait_ge(S("probsT_ready"), n + 1)
                if n >= 1:
                    act.wait_ge(S("attended"), n)
                fn(prT, ps[:, 5:8, :].rearrange("p b n -> p (b n)"), ACT.Copy).then_inc(S("probsT_copied"), 1)

            exponentials(0, m["pr"])
            turned_probs(0, m["prT"])
            act.wait_ge(S("hg_gated"), 1)
            for c in range(C):
                if c == HH:
                    act.wait_ge(S("attended_read"), 1)
                high_x(c)
            for c in range(C):
                square(2, c)
            root(2)
            high_norm(2)

            swiglu(S_FFN2, FB)
            for c in range(C):
                square(3, c)
            root(3)
            high_norm(3)

            for j in range(4):
                product(S_PLE + j)
                if j:
                    act.wait_ge(S("banks_freed"), S_PLE + j)
                fn(silu[:, :, :], pair((S_PLE + j) % BANKS), ACT.Sigmoid).then_inc(S("ple_gate"), 1)
                if j:
                    square(4, 2 * j - 2)
                    square(4, 2 * j - 1)
            square(4, C - 2)
            square(4, C - 1)
            root(4)
            for c in range(C):
                square(5, c)
            root(5)
            shift(5, 0)

            act.wait_ge(S("decay_abs"), 1)
            own(fn(fl[0:96, 1, :], fl[0:96, 1, :], ACT.Exp))
            fn(fl[0:96, 1, :], fl[0:96, 1, :], ACT.Ln, bias=1.0).then_inc(S("decay_log"), 1)

            act.wait_ge(S("padded"), 1)
            act.wait_ge(S("banks_freed"), S_IN2)
            for dst, base in ((qp, S_IN2), (kp, S_IN2 + 4)):
                for j in range(4):
                    product(base + j)
                    src = pair((base + j) % BANKS)
                    fn(dst[0:AD, 4 * j:4 * j + 4:2, :], src[0:AD, :, :], ACT.Copy)
                    copied(base + j, fn(dst[AD:P, 4 * j + 1:4 * j + 4:2, :], src[AD:P, :, :], ACT.Copy))
            for j in range(4):
                product(S_IN2 + 8 + j)
                copied(S_IN2 + 8 + j, fn(v2[:, :, j * T:(j + 1) * T], pair((S_IN2 + 8 + j) % BANKS), ACT.Copy))

            def in2_out(j):
                slot = S_IN2 + 12 + j
                product(slot)
                if j < 2:
                    copied(slot, fn(up[:, 2 * j:2 * j + 2, 16:16 + T], pair(slot % BANKS), ACT.Copy))
                else:
                    to = ga if j < 6 else gb
                    c = (j - 2) % 4 * 2
                    copied(slot, fn(to[:, c:c + 2, :], pair(slot % BANKS), ACT.Sigmoid))

            for group in range(4):
                exponentials(group + 1, s["pr"])
                in2_out(2 * group)
                in2_out(2 * group + 1)
                turned_probs(group + 1, s["prT"])
            in2_out(8)
            in2_out(9)
            act.wait_ge(S("branches"), 1)
            for c in range(C):
                high_x(c, gb)
            for c in range(C):
                square(6, c)
            root(6)
            shift(6, 3 * C)

            act.dma_start(fgrow, a["final_g"].partition_broadcast(P).rearrange("p a t -> p (a t)")
                          ).then_inc(S("final_landed"), 16)
            turned = 0

            def turned_out(to):
                nonlocal turned
                act.wait_ge(S("turned"), turned + 1)
                fn(to, ps[:, 5 + turned % 2, :], ACT.Copy).then_inc(S("turned_copied"), 1)
                turned += 1

            for hd in range(PH):
                r = (S_PQ + hd) % BANKS
                product(S_PQ + hd)
                if hd == 0:
                    act.wait_ge(S("banks_freed"), S_PQ)
                if hd >= 2:
                    act.wait_ge(S("key_scores"), hd - 1)
                fn(qT[:, hd % 2 * 2:hd % 2 * 2 + 2, :], pair(r), ACT.Copy).then_inc(S("queries_copied"), 1)
                for n in range(4):
                    if hd == 0:
                        turned_out(h2[:, n // 2, (n % 2) * 512:(n % 2 + 1) * 512])
                    if hd == 3 and n < 2:
                        turned_out(gtrow[:, n * 512:(n + 1) * 512])
                act.wait_ge(S("key_scores"), hd + 1)
                fn(scores[:, hd, :, :].rearrange("p b n -> p (b n)"), ps[:, r, :], ACT.Copy
                   ).then_inc(S("banks_freed"), 1)

            def weights(q):
                few = e["few"][:, q * 96:(q + 1) * 96]
                return {"expo": few[:, 0:16], "total": few[:, 16:17], "less": few[:, 17:18],
                        "inv": few[:, 18:19], "dots": few[:, 32:48], "act": few[:, 48:64], "w": few[:, 64:80]}

            def gate_exp(j, turn=0):
                q = j % UB
                act.wait_ge(S("chosen"), turn + (j + 1))
                top = e["vals"][:, q * 64 + 32:q * 64 + 48]
                fn(weights(q)["expo"], top, ACT.Exp, bias=weights(q)["less"], accum_out=weights(q)["total"]
                   ).then_inc(S("gates_exp"), 1)

            def activate(j, turn=0):
                w = weights(j)
                act.wait_ge(S("dotted"), turn * TK + (j + 1) * TK)
                fn(w["act"], w["dots"], ACT.Gelu).then_inc(S("gelu_ready"), 1)
                act.wait_ge(S("weights"), turn + (j + 1))
                for k in range(TK):
                    g = j * TK + k
                    if not isinstance(turn, int) or turn or g >= TK:
                        act.wait_ge(S("weighed"), turn * TK + (g - TK + 1))
                    fn(diag[:, k, :], ident, ACT.Copy, scale=w["w"][:, k:k + 1]).then_inc(S("diagonals"), 1)

            for j in range(AHEAD):
                gate_exp(j)

            def expert_turn(turn, last):
                for j in range(UB):
                    activate(j, turn)
                    if not last or j + AHEAD < UB:
                        gate_exp(j + AHEAD, turn)

            expert_turn(0, False)
            with act.Fori(1, UNITS // UB - 1) as i:
                expert_turn(i * UB, False)
            expert_turn(UNITS - UB, True)

            for b in range(TB):
                act.wait_ge(S("summed"), b + 1)
                own(fn(ubuf[:, 2 + b, :], ubuf[:, b, :], ACT.Square, accum_out=lb[:, 4 + b, 0:1]))
                fn(lb[:, 6 + b, 0:1], lb[:, 4 + b, 0:1], ACT.Sqrt, bias=eps[:, 0:1], scale=1.0 / D
                   ).then_inc(S("last_std"), 1)

        @block.vector
        def _(dve):
            v = nc.vector
            own = Chain(dve, S("dve_own"), S("dve_waited"))

            def cols(ap, n):
                return ap.unsqueeze(2).to_broadcast([ap.shape[0], ap.shape[1], n])

            def over(ap, n):
                return ap.unsqueeze(1).to_broadcast([ap.shape[0], n, ap.shape[1]])

            def inverse_std(m):
                dve.wait_ge(S("std_ready"), m + 1)
                own(v.reciprocal(rstd[:, 0, :], std[:, 0, :]))

            def norm(m, gain, to, sem):
                inverse_std(m)
                for c in range(C):
                    v.scalar_tensor_tensor(to[:, c, :], h[:, c, :], gain[:, c:c + 1], rstd[:, 0, :], ALU.mult,
                                           ALU.mult).then_inc(S(sem), 1)

            tile = 0

            def product(n, turn=0):
                nonlocal tile
                while tile < min(tiles_after(n) + TILES, 2 * W_END):
                    if on_vector(tile):
                        low(v, dve, tile, turn).then_inc(S("low_dve"), 1)
                    tile += 1
                dve.wait_ge(S("tiles_done"), turn * 2 + tiles_after(n))

            def low_x(at, x=sq):
                for c in range(C):
                    dve.wait_ge(S("high_x"), at * C + c + 1)
                    v.tensor_tensor(nl[:, c, :], x[:, c, :], nh[:, c, :].bitcast(F32), ALU.subtract
                                    ).then_inc(S("low_x"), 1)

            dve.wait_ge(S("vec_landed"), 32)
            rows = V("lb", 0, 2 * HH).rearrange("p (r h) -> p r h", r=2)
            own(v.tensor_tensor(lb[:, 4, :], rows[:, 0, :], rows[:, 1, :], ALU.max))
            v.tensor_tensor(lb[:, 0:2, :], rows, over(lb[:, 4, :], 2), ALU.subtract).then_inc(S("lb_shifted"), 1)
            dve.wait_ge(S("pos_landed"), 16)
            own(v.tensor_copy(ang[:, 1, :], posi[:, :]))
            own(v.tensor_scalar(ang[:, 0, :], ang[:, 1, :], K("inv_freq", ROPE), None, ALU.mult))
            own(v.tensor_scalar(ang[:, 1, :], ang[:, 0, :], TURN_INV, None, ALU.mult))
            own(v.tensor_scalar(ang[:, 2, :], ang[:, 1, :], ROUND, None, ALU.add))
            own(v.tensor_scalar(ang[:, 1, :], ang[:, 2, :], ROUND, None, ALU.subtract))
            for part in TURN:
                own(v.scalar_tensor_tensor(ang[:, 0, :], ang[:, 1, :], -part, ang[:, 0, :], ALU.mult, ALU.add))
            v.tensor_scalar(ang[:, 0, :], ang[:, 0, :], HALF_TURN, -HALF_TURN, ALU.min, ALU.max).then_inc(S("angle"), 1)
            low(v, dve, 0).then_inc(S("low_dve"), 1)
            tile = 2
            norm(0, V("ffn1", 0, C), sq, "normed")
            low_x(0)
            dve.wait_ge(S("sines"), 1)
            own(v.tensor_tensor(ang[:, 2, :], cos[:, :], cos[:, :], ALU.mult))
            own(v.tensor_scalar(cos[:, :], ang[:, 2, :], -2.0, 1.0, ALU.mult, ALU.add))
            dve.wait_ge(S("lb_exp"), 1)
            own(v.tensor_tensor(lb[:, 4, :], lb[:, 2, :], lb[:, 3, :], ALU.add))
            own(v.reciprocal(lb[:, 5, :], lb[:, 4, :]))
            own(v.tensor_tensor(lb[:, 0, :], lb[:, 2, :], lb[:, 5, :], ALU.mult))
            own(v.tensor_scalar(lb[:, 1, :], lb[:, 0, :], -1.0, 1.0, ALU.mult, ALU.add))

            def gated(n, b, before, turn=0):
                product(n + 1, turn)
                dve.wait_ge(S("silu_ready"), b + (before + 1))
                v.tensor_tensor(silu[:, :, :], silu[:, :, :], pair((n + 1) % BANKS), ALU.mult
                                ).then_inc(S("banks_freed"), 2)
                dve.wait_ge(S("high_gu"), b + (before + 1))
                at = slice(2 * b, 2 * b + 2) if isinstance(b, int) else bass.ds(b * 2, 2)
                v.tensor_tensor(gl[:, at, :], silu[:, :, :], gh[:, at, :].bitcast(F32), ALU.subtract
                                ).then_inc(S("low_gu"), 1)

            def weighted(j, pairs, turn=0):
                r = j % MOD_RING
                to = mod_sum[:, r, :]
                if r == 0:
                    dve.wait_ge(S("mod_read"), pairs)
                dve.wait_ge(S(f"mod_landed{r}"), turn * (16 // MOD_RING) + 16 * (j // MOD_RING + 1))
                own(v.tensor_scalar(to, wm[:, r, 0, :], V("c", 0), None, ALU.mult))
                for k in range(1, C):
                    own(v.scalar_tensor_tensor(to, wm[:, r, k, :], V("c", k), to, ALU.mult, ALU.add))
                dve.sem_inc(S("mod_summed"), 1)

            def swiglu(n, before, mod):
                nonlocal tile
                turns, pairs = FB // 2, mod // 2
                for b in range(2):
                    gated(n + 2 * b, b, before)
                    weighted(mod + b, pairs)
                tile -= 8
                with dve.Fori(1, turns) as i:
                    own.loop(i - 1, 2 * C)
                    for b in range(2):
                        gated(n + 2 * b, i * 2 + b, before, i * 4)
                        weighted(mod + b, i + pairs, i * 2)
                own.end(turns - 1)
                tile += 8 * (turns - 1)
                gated(n + 4 * turns, 2 * turns, before)
                for b in range(2):
                    weighted(mod + 2 * turns + b, turns + pairs)

            def modulated(first):
                dve.wait_ge(S("mod_read"), (first + MODS // 2) // MOD_RING)
                own(v.tensor_tensor(mod[:, 2 * first:2 * first + MODS], ps[:, 7, 2 * first:2 * first + MODS],
                                    V("b_mod", 2 * first, MODS), ALU.add))

            swiglu(S_FFN1, 0, 0)

            def half_residual(slot):
                for j in range(C):
                    product(slot + j)
                    v.scalar_tensor_tensor(h[:, j, :], ps[:, (slot + j) % BANKS, 0:T], 0.5, h[:, j, :], ALU.mult,
                                           ALU.add).then_inc(S("banks_freed"), 1)

            half_residual(S_DOWN1)
            norm(1, V("mix", 0, C), sq, "normed")
            low_x(1)
            modulated(0)

            f = heads(m["b0"], HH)
            raw = heads(m["b1"], HH)
            for hd in range(HH):
                if hd % 2 == 0:
                    dve.wait_ge(S("banks_freed"), S_IN + hd // 2 + 1)
                one_less, least = lb[:, 1, hd:hd + 1], lb[:, 0, hd:hd + 1]
                v.tensor_scalar(f[:, hd, :], raw[:, hd, :], one_less, least, ALU.mult, ALU.add)
                own(v.tensor_scalar(hk[:, hd, :], hk[:, hd, :], one_less, None, ALU.mult))
            dve.wait_ge(S("banks_freed"), S_IN + 4)
            v.tensor_tensor(m["qf"], m["q"], m["b0"], ALU.mult).then_inc(S("level_operands"), 2)
            dve.wait_ge(S("small_landed"), 16 * 5)
            dve.wait_ge(S("scores_zeroed"), 1)

            def level_read(n):
                dve.wait_ge(S("level_ready"), n + 1)
                v.copy_predicated(m["sc"].rearrange("p (x t) -> p x t", x=2 * HH),
                                  over(lev_mask[:, n, :], 2 * HH),
                                  ps[:, 4:6, :].rearrange("p b n -> p (b n)").rearrange("p (x t) -> p x t", x=2 * HH)
                                  ).then_inc(S("level_read"), 1)

            def widen(n):
                z = 2 ** n
                src, dst = m[f"b{n % 2}"], m[f"b{(n + 1) % 2}"]
                blocks = HH * T // z
                whole = src[:, 0:blocks].rearrange("p (n two) -> p n two", two=2)
                qv = m["qf"].rearrange("p (n two z) -> p n two z", two=2, z=z)
                kv = m["k"].rearrange("p (n two z) -> p n two z", two=2, z=z)
                own(v.tensor_tensor(dst[:, 0:blocks // 2], whole[:, :, 0], whole[:, :, 1], ALU.mult))
                v.tensor_tensor(qv[:, :, 1, :], qv[:, :, 1, :], cols(whole[:, :, 0], z), ALU.mult)
                own(v.tensor_tensor(kv[:, :, 0, :], kv[:, :, 0, :], cols(whole[:, :, 1], z), ALU.mult))
                dve.sem_inc(S("level_operands"), 1)

            level_read(0)
            level_read(1)
            widen(0)

            def latent_inverse():
                dve.wait_ge(S("latent_copied"), 1)
                own(v.reciprocal(rstd[:, :, :].rearrange("p a t -> p (a t)"), std[:, :, :].rearrange("p a t -> p (a t)")))
                for k in range(2):
                    last = v.scalar_tensor_tensor(cqn[:, k, :], cq[:, k, :], V("q_a", k), rstd[:, 0, :], ALU.mult, ALU.mult)
                last.then_inc(S("latent_normed"), 1)
                v.scalar_tensor_tensor(cqn[:, 2, :], cq[:, 2, :], V("kv_a"), rstd[:, 1, :], ALU.mult, ALU.mult
                                       ).then_inc(S("latent_normed"), 1)

            latent_inverse()
            for n in range(2, LEVELS + 1):
                level_read(n)
                widen(n - 1)
                if n == 4:
                    dve.wait_ge(S("latent_copied"), 5)
                    v.tensor_tensor(rt[0:ROPE, :, :], xr[0:ROPE, :, :], over(cos[:, :], HH + 1), ALU.mult)
                if n >= 5:
                    j = (n - 5) * 2
                    k = min(2, HH + 1 - j)
                    dve.wait_ge(S("latent_ready"), 10 + n - 5)
                    own(v.tensor_tensor(rot[0:ROPE, j:j + k, :],
                                        ps[0:ROPE, 6 + (n - 5 + 9) % 2, 0:k * T].rearrange("p (t n) -> p t n", t=k),
                                        over(sin[:, :], k), ALU.mult))
                    dve.sem_inc(S("rotated"), 1)
            dve.wait_ge(S("level_ready"), LEVELS + 2)
            v.tensor_copy(m["sc7"], ps[:, 4, :]).then_inc(S("scores_built"), 1)
            v.tensor_tensor(rot[0:ROPE, :, :], rot[0:ROPE, :, :], rt[0:ROPE, :, :], ALU.add).then_inc(S("rope_done"), 1)

            causal = K("causal")

            def softmax(n, pr, st, scale):
                p0 = pr[:, 0:512].rearrange("p (h t) -> p h t", h=4)
                p1 = pr[:, 512:1536].rearrange("p (h t) -> p h t", h=4)
                dve.wait_ge(S("scores_ready"), n + 1)
                if n >= 2:
                    dve.wait_ge(S("probsT_ready"), n)
                v.scalar_tensor_tensor(p0, ps[:, 5, :].rearrange("p (h t) -> p h t", h=4), scale,
                                       over(causal[:, P:2 * P], 4), ALU.mult, ALU.add)
                own(v.scalar_tensor_tensor(p1, ps[:, 6:8, :].rearrange("p b n -> p (b n)").rearrange(
                    "p (h t) -> p h t", h=4), scale, over(causal, 4), ALU.mult, ALU.add))
                v.tensor_reduce(st[:, 0:4], p0, AX, ALU.max)
                own(v.tensor_reduce(st[:, 4:8], p1, AX, ALU.max))
                v.tensor_tensor(p0, p0, cols(st[:, 0:4], P), ALU.subtract)
                own(v.tensor_tensor(p1, p1, cols(st[:, 4:8], T), ALU.subtract))
                dve.sem_inc(S("logits"), 1)

            def normalise(n, pr, st):
                p0 = pr[:, 0:512].rearrange("p (h t) -> p h t", h=4)
                p1 = pr[:, 512:1536].rearrange("p (h t) -> p h t", h=4)
                dve.wait_ge(S("probs_exp"), n + 1)
                v.tensor_reduce(st[:, 8:12], p0, AX, ALU.add)
                own(v.tensor_reduce(st[:, 12:16], p1, AX, ALU.add))
                own(v.reciprocal(st[:, 16:24], st[:, 8:16]))
                v.tensor_tensor(p0, p0, cols(st[:, 16:20], P), ALU.mult)
                own(v.tensor_tensor(p1, p1, cols(st[:, 20:24], T), ALU.mult))
                dve.sem_inc(S("probs_ready"), 1)

            softmax(0, m["pr"], m["st"], float(QK) ** -0.5)
            dve.wait_ge(S("hg_std"), 1)
            own(v.reciprocal(osq[:, 0:2, :], ostd[:, 0:2, :]))
            normalise(0, m["pr"], m["st"])
            own(v.reciprocal(osq[:, 2:HH, :], ostd[:, 2:HH, :]))
            dve.wait_ge(S("hg_copied"), 1)
            for hd in range(HH):
                ins = v.scalar_tensor_tensor(ho[:, hd, :], ho[:, hd, :], V("hg_norm", hd), osq[:, hd, :], ALU.mult, ALU.mult)
            own(ins)
            v.tensor_tensor(mixed[:, 0:HH, :], ho[:, :, :], hg[:, :, :], ALU.mult).then_inc(S("hg_gated"), 1)
            dve.wait_ge(S("attended"), 1)
            v.tensor_copy(mixed[:, HH:C, :].rearrange("p h t -> p (h t)"), ps[:, 5:7, :].rearrange("p b n -> p (b n)")
                          ).then_inc(S("attended_read"), 1)

            dve.wait_ge(S("banks_freed"), S_OUT)
            low_x(2)
            for j in range(4):
                product(S_OUT + j)
                v.tensor_tensor(h[:, 2 * j:2 * j + 2, :], pair((S_OUT + j) % BANKS), h[:, 2 * j:2 * j + 2, :], ALU.add
                                ).then_inc(S("banks_freed"), 1)
            norm(2, V("ffn2", 0, C), sq, "normed")
            low_x(3)
            swiglu(S_FFN2, FB, MODS // 2)
            half_residual(S_DOWN2)
            norm(3, V("ple", 0, C), sq, "normed")
            low_x(4)
            modulated(MODS // 2)

            for j in range(4):
                product(S_PLE + j)
                dve.wait_ge(S("ple_gate"), j + 1)
                dve.wait_ge(S("ple_ready"), j + 1)
                own(v.tensor_tensor(silu[:, :, :], silu[:, :, :], ps[:, 5 + j % 2, :].rearrange("p (t n) -> p t n", t=2),
                                    ALU.mult))
                v.tensor_tensor(h[:, 2 * j:2 * j + 2, :], silu[:, :, :], h[:, 2 * j:2 * j + 2, :], ALU.add
                                ).then_inc(S("banks_freed"), 1)
                dve.sem_inc(S("ple_added"), 1)
            norm(4, V("final1", 0, C), h, "block1_out")

            def modulated_norm(m, gain, scale_at):
                co = coef[:, 0:C]
                own(v.tensor_scalar(coef[:, C:2 * C], mod[:, scale_at:scale_at + C], 1.0, None, ALU.add))
                own(v.tensor_tensor(co, coef[:, C:2 * C], gain, ALU.mult))
                norm(m, co, sq, "scaled")

            modulated_norm(5, V("norm1", 0, C), C)
            low_x(5)

            dve.wait_ge(S("forget_ready"), 1)
            own(v.tensor_scalar(fl[0:96, 0, :], ps[0:96, 5, 0:T], vec[0:96, slice(*VEC["b_f"])], None, ALU.add))
            own(v.tensor_scalar(fl[0:96, 2, :], fl[0:96, 0, :], -1.0, None, ALU.mult))
            v.tensor_tensor(fl[0:96, 1, :], fl[0:96, 0, :], fl[0:96, 2, :], ALU.min).then_inc(S("decay_abs"), 1)
            dve.wait_ge(S("decay_abs"), 1)
            own(v.tensor_scalar(fl[0:96, 2, :], fl[0:96, 0, :], 0.0, None, ALU.min))
            own(v.memset(fl[0:96, 3, :], 1.0))
            dve.wait_ge(S("decay_log"), 1)
            own(v.tensor_tensor(fl[0:96, 0, :], fl[0:96, 2, :], fl[0:96, 1, :], ALU.subtract))
            own(v.tensor_tensor_scan(fl[0:96, 4, :], fl[0:96, 3, :], fl[0:96, 0, :], 0.0, ALU.mult, ALU.add))
            unscale = float(AD) ** 0.5
            own(v.tensor_scalar(fl[0:96, 0, :], fl[0:96, 4, :], K("is_value", 96), unscale, ALU.mult, ALU.mult))
            own(v.tensor_scalar(fl[0:96, 1, :], fl[0:96, 4, :], K("not_value", 96), -unscale, ALU.mult, ALU.mult))
            dve.wait_ge(S("padded"), 1)
            for row, odd in ((AD, 0), (0, 1)):
                rs = slice(row, row + 32)
                for dst, src, sel in ((qp, 0, "sel_q"), (kp, 1, "sel_k")):
                    v.tensor_tensor(dst[rs, odd:AH:2, :], over(fl[rs, src, :], AH // 2),
                                    cols(con[rs, CON[sel][0] + odd:CON[sel][1]:2], T), ALU.add
                                    ).then_inc(S("decay_rows"), 1)

            for group in range(4):
                n = group + 1
                softmax(n, s["pr"], s["st"], float(AD) ** -0.5)
                normalise(n, s["pr"], s["st"])
                dve.wait_ge(S("attended"), n + 1)
                v.tensor_copy(o2[:, 2 * group:2 * group + 2, :].rearrange("p c t -> p (c t)"), ps[:, 4, :]
                              ).then_inc(S("attended_read"), 1)

            dve.wait_ge(S("banks_freed"), S_OUT2)
            for c in range(C):
                g, t = c // 2, c % 2
                if t == 0:
                    dve.wait_ge(S("pool_ready"), g + 1)
                ins = v.scalar_tensor_tensor(ga[:, c, :], ps[:, 5 + g % 2, t * T:(t + 1) * T], V("pool_scale", c),
                                             ga[:, c, :], ALU.mult, ALU.mult)
                if t == 1:
                    ins.then_inc(S("pool_read"), 1)
            dve.wait_ge(S("attended_read"), 5)
            own(v.tensor_tensor(gb[:, :, :], gb[:, :, :], o2[:, :, :], ALU.mult))
            dve.wait_ge(S("pool_read"), 4)
            v.tensor_tensor(gb[:, :, :], gb[:, :, :], ga[:, :, :], ALU.add).then_inc(S("branches"), 1)

            low_x(6, gb)
            for j in range(4):
                product(S_OUT2 + j)
                for t in range(2):
                    c = 2 * j + t
                    ins = v.scalar_tensor_tensor(h[:, c, :], pair((S_OUT2 + j) % BANKS)[:, t, :],
                                                 mod[:, 2 * C + c:2 * C + c + 1], h[:, c, :], ALU.mult, ALU.add)
                ins.then_inc(S("banks_freed"), 1)
            modulated_norm(6, V("norm2", 0, C), 4 * C)
            low_x(7)
            v.tensor_tensor(gtb, cols(mod[:, 5 * C:6 * C], P),
                            ones[:, :].unsqueeze(1).to_broadcast([P, C, P]), ALU.mult).then_inc(S("gate_columns"), 1)

            iota = K("iota")

            def top16(values, to_values, to_index, work):
                own(v.max(to_values[:, 0:8], values), apart=True)
                v.max_index(to_index[:, 0:8], to_values[:, 0:8], values)
                own(v.match_replace(work, to_values[:, 0:8], values, NEG), apart=True)
                own(v.max(to_values[:, 8:16], work), apart=True)
                own(v.max_index(to_index[:, 8:16], to_values[:, 8:16], work), apart=True)

            def choose(j, head, turn=0):
                q, b = j % UB, j % TB
                vals = e["vals"][:, q * 64:(q + 1) * 64]
                few = e["few"][:, q * 96:(q + 1) * 96]
                work, index = e["wk"], e["sel"].bitcast(U32)
                dve.wait_ge(S("banks_freed"), head + (S_PQ + 1))
                src = scores[:, head, b, :] if isinstance(head, int) else \
                    scores[:, bass.ds(head, 1), b, :].rearrange("p a n -> p (a n)")
                own(v.tensor_copy(work[:, 0:256], src), apart=True)
                for p in range(2):
                    top16(work[:, p * NK:(p + 1) * NK], vals[:, p * 16:(p + 1) * 16], index[:, p * 16:(p + 1) * 16],
                          work[:, 256:256 + NK])
                own(v.tensor_copy(work[:, 512:544], index))
                cand = work[:, 0:256]
                own(v.tensor_tensor(cand.rearrange("p (i j) -> p i j", i=TK), cols(vals[:, 0:TK], TK),
                                    over(vals[:, TK:2 * TK], TK), ALU.add), apart=True)
                top16(cand, vals[:, 32:48], index[:, 0:16], work[:, 256:512])
                own(v.tensor_scalar(few[:, 17:18], vals[:, 32:33], -1.0, None, ALU.mult))
                dve.sem_inc(S("chosen"), 1)
                own(v.tensor_scalar(index[:, 16:32], index[:, 0:16], TK - 1, None, ALU.bitwise_and))
                own(v.tensor_scalar(index[:, 0:16], index[:, 0:16], 4, None, ALU.logical_shift_right))
                own(v.tensor_copy(work[:, 544:576], index))
                hot = e["oh"].rearrange("p (k j) -> p k j", j=TK)
                own(v.tensor_tensor(hot, cols(work[:, 544:576], TK), over(iota, 2 * TK), ALU.is_equal))
                hot4 = e["oh"].rearrange("p (s k j) -> p s k j", s=2, j=TK)
                lists = work[:, 512:544].rearrange("p (s j) -> p s j", s=2).unsqueeze(2).to_broadcast([P, 2, TK, TK])
                own(v.tensor_tensor(hot4, hot4, lists, ALU.mult))
                own(v.tensor_reduce(work[:, 576:608], hot, AX, ALU.add))
                if j >= UB or not isinstance(turn, int):
                    dve.wait_ge(S("weighed"), turn * TK + (j - UB + 1) * TK)
                v.scalar_tensor_tensor(few[:, 80:96].bitcast(U32), work[:, 576:592], float(NK), work[:, 592:608],
                                       ALU.mult, ALU.add).then_inc(S("indices"), 1)

            def dots(j, turn=0):
                b = j % TB
                few = e["few"][:, j * 96:(j + 1) * 96]
                for k in range(TK):
                    g = j * TK + k
                    dve.wait_ge(S(f"u_landed{g % RU}"), turn * (TK * 16 // RU) + 16 * (g // RU + 1))
                    own(v.tensor_tensor_reduce(out=e["junk"], in0=ubuf[:, g % RU, :], in1=h2[:, b, :], scale=1.0,
                                               scalar=0.0, op0=ALU.mult, op1=ALU.add, accum_out=few[:, 32 + k:33 + k]))
                    dve.sem_inc(S("dotted"), 1)

            def weigh(j, turn=0):
                few = e["few"][:, j * 96:(j + 1) * 96]
                dve.wait_ge(S("gates_exp"), turn + (j + 1))
                own(v.reciprocal(few[:, 18:19], few[:, 16:17]))
                dve.wait_ge(S("gelu_ready"), turn + (j + 1))
                v.scalar_tensor_tensor(few[:, 64:80], few[:, 48:64], few[:, 18:19], few[:, 0:16], ALU.mult, ALU.mult
                                       ).then_inc(S("weights"), 1)

            dve.wait_ge(S("turned_copied"), 4)
            for j in range(AHEAD):
                choose(j, j // TB)

            def expert_turn(i, last):
                turn = i * UB
                for j in range(UB):
                    dots(j, turn)
                    weigh(j, turn)
                    if not last or j + AHEAD < UB:
                        choose(j + AHEAD, i * (UB // TB) + (j + AHEAD) // TB, turn)

            turns = UNITS // UB
            before = own.n
            expert_turn(0, False)
            per_turn = own.n - before
            with dve.Fori(1, turns - 1) as i:
                own.loop(i - 1, per_turn)
                expert_turn(i, False)
            own.end(turns - 2)
            expert_turn(turns - 1, True)

            dve.wait_ge(S("turned_copied"), 6)
            dve.wait_ge(S("residual_turned"), 1)
            dve.wait_ge(S("final_landed"), 16)
            for b in range(TB):
                dve.wait_ge(S("weighed"), UNITS * TK - (TB - 1 - b) * TK)
                own(v.tensor_tensor(e["junk"], ps[:, 4 + 2 * b:6 + 2 * b, :].rearrange("p a n -> p (a n)"), gtrow, ALU.mult))
                v.tensor_tensor(ubuf[:, b, :], e["junk"], ps[:, 2 * b:2 * b + 2, :].rearrange("p a n -> p (a n)"), ALU.add).then_inc(S("summed"), 1)
                dve.wait_ge(S("last_std"), b + 1)
                own(v.reciprocal(lb[:, 6 + b, 1:2], lb[:, 6 + b, 0:1]))
                v.scalar_tensor_tensor(ubuf[:, b, :], ubuf[:, b, :], lb[:, 6 + b, 1:2], fgrow, ALU.mult, ALU.mult
                                       ).then_inc(S("out_ready"), 1)

        @block.gpsimd
        def _(pool):
            g = nc.gpsimd
            own = Chain(pool, S("pool_own"), S("pool_waited"))
            g.memset(eps[:, :], EPS)
            g.memset(zeros[:, :], 0.0)
            g.memset(ones[:, :], 1.0).then_inc(S("constants"), 2)

            def split(n, upto):
                for tile in range(2 * weight_slot(n), 2 * weight_slot(upto)):
                    if not on_vector(tile):
                        low(g, pool, tile).then_inc(S("low_pool"), 1)

            def swiglu(n):
                turns = FB // 2
                with pool.Fori(0, turns) as i:
                    for tile in range(2 * weight_slot(n) + 1, 2 * weight_slot(n + 4), 2):
                        low(g, pool, tile, i * 4).then_inc(S("low_pool"), 1)
                split(n + 4 * turns, n + 2 * FB)

            swiglu(S_FFN1)
            split(S_DOWN1, S_IN + 2)
            pool.wait_ge(S("tiles_done"), tiles_after(S_IN - 1))
            g.memset(m["sc"], 0.0).then_inc(S("scores_zeroed"), 1)
            split(S_IN + 2, S_FFN2)
            swiglu(S_FFN2)
            split(S_DOWN2, S_PLE + 2)

            pool.wait_ge(S("tiles_done"), tiles_after(S_PLE - 1))
            g.memset(s["qp"], 0.0)
            split(S_PLE + 2, S_PLE + 3)
            own(g.memset(s["kp"], 0.0))
            split(S_PLE + 3, S_IN2 + 2)
            pool.wait_ge(S("ple_ready"), 4)
            for name in ("up", "s1", "s2", "s4", "s8"):
                last = g.memset(s[name], 0.0)
            own(last)
            pool.sem_inc(S("padded"), 1)
            split(S_IN2 + 2, S_IN2 + 16)

            pool.wait_ge(S("small_landed"), 16 * 5)
            pool.wait_ge(S("banks_freed"), S_IN2 + 14)
            t0 = 16
            n = S_IN2 + 16
            for dst, src, first, lag in ((s1, up, 0, 1), (s2, s1, 1, 2), (s4, s2, 1, 4), (s8, s4, 1, 8)):
                groups = dst.shape[1]
                own(g.tensor_tensor(dst[:, :, t0:t0 + T], src[:, first:first + groups, t0:t0 + T],
                                    src[:, first:first + groups, t0 - lag:t0 - lag + T], ALU.add))
                split(n, n + 1)
                n += 1
            for k, src in enumerate((s1, s2, s4, s8)):
                own(g.tensor_tensor(pooled[:, k, :], src[:, 0, t0:t0 + T], inv_count[:, k, :], ALU.mult))
            split(n, n + 1)
            g.tensor_tensor(pooled[:, :, :], pooled[:, :, :], up[:, :, t0:t0 + T], ALU.subtract).then_inc(S("pooled"), 1)
            split(n + 1, S_PQ + AHEAD_Q)

            def fetch(j, turn, table, to, ring_size, landed, used, rows, between={}):
                q = j % UB
                few = e["few"][:, q * 96:(q + 1) * 96]
                pool.wait_ge(S("indices"), turn + (j + 1))
                for k in rows:
                    row = j * TK + k
                    if not (isinstance(turn, int) and turn * TK + row < ring_size):
                        pool.wait_ge(S(used), turn * TK + (row - ring_size + 1))
                        own.apart()
                    g.indirect_dma_start(to[:, row % ring_size, :], None, table,
                                         bass.IndirectOffsetOnAxis(ap=few[:, 80 + k:81 + k].bitcast(U32), axis=0)
                                         ).then_inc(S(f"{landed}{row % ring_size}"), 16)
                    if k in between:
                        split(between[k], between[k] + 1)

            def fetch_u(j, turn=0, rows=range(TK), between={}):
                fetch(j, turn, a["expert_u"], ubuf, RU, "u_landed", "dotted", rows, between)

            def fetch_v(j, turn=0, rows=range(TK)):
                fetch(j, turn, a["expert_v"], vbuf, RV, "v_landed", "weighed", rows)

            def expert_turn(turn, last, first=0):
                for j in range(first, UB):
                    if not last or j + 1 < UB:
                        fetch_u(j + 1, turn)
                    fetch_v(j, turn)

            late = list(range(S_PQ + AHEAD_Q, S_END))
            fetch_u(0, between={4 * i + 3: n for i, n in enumerate(late)})
            fetch_u(1, rows=range(RU))
            pool.wait_ge(S("tiles_done"), 2 * W_END)
            fetch_v(0, rows=range(RV))
            fetch_u(1, rows=range(RU, TK))
            fetch_v(0, rows=range(RV, TK))
            expert_turn(0, False, 1)
            with pool.Fori(1, UNITS // UB - 1) as i:
                expert_turn(i * UB, False)
            expert_turn(UNITS - UB, True)


TURN = (6.28125, 0.0019350051879882812, 3.01991598e-07)
TURN_INV = float(1.0 / (2.0 * np.pi))
HALF_TURN = 3.1415925
ROUND = float(1.5 * 2 ** 23)


def constants():
    con = np.zeros((P, N_CON), np.float32)

    def put(name, value, rows=P):
        con[:rows, CON[name][0]:CON[name][1]] = value

    put("ident", np.eye(P))
    swap = np.zeros((ROPE, ROPE))
    half = ROPE // 2
    for i in range(half):
        swap[i + half, i] = -1.0
        swap[i, i + half] = 1.0
    put("swap", swap, ROPE)
    tri = np.where(np.arange(P)[:, None] >= np.arange(P)[None, :], 0.0, NEG)
    put("causal", np.concatenate([np.zeros((P, P)), tri], 1))
    put("iota", np.arange(TK)[None, :])
    inv = (10000.0 ** (-np.arange(half, dtype=np.float64) / half)).astype(np.float32)
    put("inv_freq", np.concatenate([inv, inv])[:, None], ROPE)
    rows = np.arange(P) % 64
    put("is_value", (rows < AH)[:, None].astype(np.float32))
    put("not_value", ((rows >= AH) & (rows < 2 * AH))[:, None].astype(np.float32))
    put("sel_q", (rows[:, None] == AH + np.arange(AH)[None, :]).astype(np.float32))
    put("sel_k", (rows[:, None] == np.arange(AH)[None, :]).astype(np.float32))

    at = np.arange(P)
    masks = np.zeros((P, LEVELS + 1, P), np.int32)
    masks[:, 0] = np.eye(P)
    for n in range(LEVELS):
        sb, tb = at[:, None] >> n, at[None, :] >> n
        masks[:, n + 1] = (sb % 2 == 0) & (tb == sb + 1)
    inv_count = np.stack([1.0 / np.minimum(np.arange(T) + 1, 2 ** (g + 1)) for g in range(4)]).astype(np.float32)
    return con, masks, inv_count.reshape(1, 4 * T)


def kernel(**inputs):
    import concourse.bacc as bacc
    from concourse.bass_utils import run_bass_kernel_spmd

    x = {k: np.asarray(v) for k, v in inputs.items()}

    def slots(w, width=T):
        k, n = w.shape[0] // P, w.shape[1] // width
        return w.reshape(k, P, n, width).transpose(2, 1, 0, 3).reshape(n, P, k * width)

    def by_feature(w):
        return w.reshape(-1, P).T

    def blocks(w):
        k, n = w.shape[0] // P, w.shape[1] // P
        return w.reshape(k, P, n, P).transpose(2, 0, 1, 3).reshape(n * k, P, P)

    w_in, w_in2 = x["w_in"][0], x["w_in_2"][0]
    def gate_up(gate, up):
        both = [blocks(w[0]).reshape(FB, 2 * C, P, P) for w in (gate, up)]
        return np.stack(both, 1).reshape(-1, P, P)

    latent = np.concatenate([w_in[:, 2048:2496], np.zeros((D, 64), np.float32)], 1)
    stream = [
        gate_up(x["w1_gate"], x["w1_up"]), blocks(x["w1_down"][0]),
        blocks(np.concatenate([w_in[:, 512:1024], w_in[:, 0:512], latent, w_in[:, 1024:2048]], 1)),
        blocks(x["w_out"][0]),
        gate_up(x["w2_gate"], x["w2_up"]), blocks(x["w2_down"][0]),
        blocks(x["w_ple_gate"][0]),
        blocks(np.concatenate([w_in2[:, 512:3584], w_in2[:, 0:512], w_in2[:, 3600:5648]], 1)),
        blocks(x["w_out_2"][0]), blocks(x["peer_w_query_2"][0]),
    ]
    stream = np.concatenate(stream).reshape(W_END, 2 * C, P, P).transpose(0, 2, 1, 3).reshape(W_END, P, SLOT)

    con, masks, inv_count = constants()
    f_cols = w_in2[:, 3584:3600]
    wf = np.zeros((D, 96), np.float32)
    b_f = np.zeros((P, 1), np.float32)
    for at in (0, 16, 64, 80):
        wf[:, at:at + AH] = f_cols
        b_f[at:at + AH, 0] = x["b_f_2"][0]
    table = {"ffn1": "ln_ffn1", "mix": "ln_mix", "ffn2": "ln_ffn2", "ple": "ln_ple", "final1": "ln_final",
             "norm1": "norm1_g_2", "norm2": "norm2_g_2", "pool_scale": "pool_scale_2", "hg_norm": "hg_out_norm",
             "q_a": "q_a_norm", "kv_a": "kv_a_norm", "lb": "hg_lb_logits", "c": "c_2", "b_mod": "b_mod_2"}
    vec = np.concatenate([b_f if n == "b_f" else by_feature(x[table[n]]) for n in VEC], 1)
    small = np.concatenate([slots(x["w_q_up"][0], HH * QK)[0], x["w_kv_up"][0], slots(x["w_ple_proj"][0], D)[0],
                            x["w_pool_2"][0].transpose(1, 0, 2).reshape(P, 4 * T)], 1)
    arrays = {
        "x": slots(x["x"][0].T)[0].reshape(P, C, T),
        "p": slots(x["p"][0, 0].T)[0].reshape(P, 2, T),
        "pos": x["positions"].reshape(1, T).astype(np.int32),
        "vec": vec, "con": con, "lev_mask": masks, "inv_count": inv_count,
        "w": stream, "wmod": slots(x["w_mod_2"][0]), "small": small,
        "wf": slots(wf, 96)[0].reshape(P, C, 96),
        "keys": x["peer_sub_keys_2"][0].reshape(2 * PH, NK, P).transpose(2, 0, 1),
        "expert_u": x["peer_u_2"][0], "expert_v": x["peer_v_2"][0],
        "final_g": x["final_g_2"].reshape(1, D),
    }
    nc = bacc.Bacc("TRN2", target_bir_lowering=False, num_devices=1)
    feeds, aps = {}, {}
    for name, value in arrays.items():
        value = np.ascontiguousarray(value)
        feeds[f"in_{name}"] = value
        aps[name] = nc.dram_tensor(f"in_{name}", value.shape, mybir.dt.from_np(value.dtype), kind="ExternalInput").ap()
    out = nc.dram_tensor("out", (T, D), F32, kind="ExternalOutput").ap()
    program(nc, aps, out)
    result = run_bass_kernel_spmd(nc, [feeds], core_ids=[0])
    return result.results[0]["out"].reshape(1, T, D)
```
